# Optimizing a Trainium2 kernel written in Bass

```python
import jax, jax.numpy as jnp
from jax import lax
import numpy as np
import math

D_MODEL = 1024
BATCH = 1
SEQ = 512
DEPTH = 2

GRID_W = 64
CTX_LEN = 256
N_EVEN = (DEPTH + 1) // 2
N_ODD = DEPTH // 2
EPS = 1e-6

ML_HEADS = 4
ML_DK = 64
ML_DV = 128
ML_CHUNK = 64
SC_WIDTH = D_MODEL // 2
CONV_K = 3
HYB_SIZES = (ML_HEADS * ML_DK, ML_HEADS * ML_DK, ML_HEADS * ML_DV, ML_HEADS * ML_DV, 4 * ML_HEADS, SC_WIDTH, SC_WIDTH, SC_WIDTH)
HYB_IN = sum(HYB_SIZES)
HYB_OUT = ML_HEADS * ML_DV + SC_WIDTH
ATT_HEADS = 16
KV_HEADS = 4
HEAD_DIM = 64
ATT_IN = (ATT_HEADS + 2 * KV_HEADS) * HEAD_DIM
Q_BLOCK = 128
ROPE_THETA = 10000.0
MLP_HIDDEN = 4 * D_MODEL


def rms_norm(x, g):
    xf = x.astype(jnp.float32)
    y = xf * lax.rsqrt(jnp.mean(xf * xf, axis=-1, keepdims=True) + EPS)
    return (y * g.astype(jnp.float32)).astype(x.dtype)

def sqrelu_mlp(h, w1, w2):
    return jnp.square(jax.nn.relu(h @ w1)) @ w2

def axial_rope_tables(n_rows):
    half = HEAD_DIM // 2
    inv = ROPE_THETA ** (-jnp.arange(0, half, 2, dtype=jnp.float32) / half)
    t = jnp.arange(n_rows * GRID_W)
    row = (t // GRID_W).astype(jnp.float32)
    col = (t % GRID_W).astype(jnp.float32)
    ang = jnp.concatenate([row[:, None] * inv, col[:, None] * inv], axis=-1)
    return jnp.cos(ang), jnp.sin(ang)

def _rotate_half(part, cs, sn):
    n = part.shape[-1] // 2
    p1, p2 = part[..., :n], part[..., n:]
    return jnp.concatenate([p1 * cs - p2 * sn, p2 * cs + p1 * sn], axis=-1)

def apply_axial_rope(x, cos, sin):
    half, quarter = HEAD_DIM // 2, HEAD_DIM // 4
    xf = x.astype(jnp.float32)
    cs, sn = cos[None, :, None, :], sin[None, :, None, :]
    row = _rotate_half(xf[..., :half], cs[..., :quarter], sn[..., :quarter])
    col = _rotate_half(xf[..., half:], cs[..., quarter:], sn[..., quarter:])
    return jnp.concatenate([row, col], axis=-1).astype(x.dtype)

def mlstm_chunk_states(k, v, ig, lf, state0):
    b = jnp.cumsum(lf, axis=-1)
    b_end = b[..., -1]
    logw = b_end[..., None] - b + ig
    m_loc = jnp.max(logw, axis=-1)
    w = jnp.exp(logw - m_loc[..., None])
    c_loc = jnp.einsum('bhcsv,bhcsk->bhcvk', v * w[..., None], k)
    n_loc = jnp.einsum('bhcs,bhcsk->bhck', w, k)

    def step(carry, inp):
        c_st, n_st, m_st = carry
        bl, ml, cl, nl = inp
        m_new = jnp.maximum(bl + m_st, ml)
        a = jnp.exp(bl + m_st - m_new)
        g = jnp.exp(ml - m_new)
        c_new = a[..., None, None] * c_st + g[..., None, None] * cl
        n_new = a[..., None] * n_st + g[..., None] * nl
        return (c_new, n_new, m_new), (c_st, n_st, m_st)

    xs = tuple(jnp.moveaxis(t, 2, 0) for t in (b_end, m_loc, c_loc, n_loc))
    final, starts = lax.scan(step, state0, xs)
    starts = tuple(jnp.moveaxis(t, 0, 2) for t in starts)
    return starts, final

def mlstm_chunk_outputs(q, k, v, ig, lf, starts):
    c0, n0, m0 = starts
    b = jnp.cumsum(lf, axis=-1)
    length = q.shape[-2]
    tri = jnp.tril(jnp.ones((length, length), dtype=bool))
    log_d = jnp.where(tri, b[..., :, None] - b[..., None, :] + ig[..., None, :], -jnp.inf)
    m_inter = b + m0[..., None]
    m = jnp.maximum(m_inter, jnp.max(log_d, axis=-1))
    d = jnp.exp(log_d - m[..., None])
    a = jnp.exp(m_inter - m)
    s = jnp.einsum('bhcjd,bhcsd->bhcjs', q, k) * d
    num = jnp.einsum('bhcjs,bhcsv->bhcjv', s, v) + a[..., None] * jnp.einsum('bhcvd,bhcjd->bhcjv', c0, q)
    den = jnp.sum(s, axis=-1) + a * jnp.einsum('bhcd,bhcjd->bhcj', n0, q)
    return num / jnp.maximum(jnp.abs(den), jnp.exp(-m))[..., None]

def mlstm_direction(q, k, v, ig, lf, state0, reverse, need_h):
    if reverse:
        q, k, v, ig, lf = (jnp.flip(t, axis=2) for t in (q, k, v, ig, lf))
    bsz, nh, n, _ = q.shape
    nc = n // ML_CHUNK
    chunk = lambda t: t.reshape(bsz, nh, nc, ML_CHUNK, *t.shape[3:])
    q, k, v, ig, lf = (chunk(t) for t in (q, k, v, ig, lf))
    starts, final = mlstm_chunk_states(k, v, ig, lf, state0)
    if not need_h:
        return None, final
    h = mlstm_chunk_outputs(q, k, v, ig, lf, starts).reshape(bsz, nh, n, ML_DV)
    if reverse:
        h = jnp.flip(h, axis=2)
    return h, final

def short_conv(u, w):
    return lax.conv_general_dilated(u, w[:, None, :].astype(u.dtype), window_strides=(1,),
                                    padding=[(CONV_K // 2, CONV_K // 2)],
                                    dimension_numbers=('NWC', 'WIO', 'NWC'),
                                    feature_group_count=u.shape[-1])

def hybrid_mixer(hc, hx, w_in, gate_b, mnorm_g, conv_w, w_out, with_ctx):
    splits = np.cumsum(HYB_SIZES)[:-1].tolist()

    def project(h):
        bsz, n, _ = h.shape
        q, k, v, o, g, gb, gc, u = jnp.split(h @ w_in, splits, axis=-1)
        heads = lambda t, dd: t.reshape(bsz, n, ML_HEADS, dd).transpose(0, 2, 1, 3).astype(jnp.float32)
        g = (g.astype(jnp.float32) + gate_b.astype(jnp.float32)).reshape(bsz, n, 4, ML_HEADS).transpose(2, 0, 3, 1)
        fwd = (g[0], jax.nn.log_sigmoid(g[1]))
        bwd = (g[2], jax.nn.log_sigmoid(g[3]))
        qkv = (heads(q, ML_DK) * ML_DK ** -0.5, heads(k, ML_DK), heads(v, ML_DV))
        return qkv, fwd, bwd, (o, gb, gc, u)

    def combine(h, side):
        o, gb, gc, u = side
        bsz, n, _ = o.shape
        hn = rms_norm(h.transpose(0, 2, 1, 3), mnorm_g.reshape(ML_HEADS, ML_DV))
        og = jax.nn.sigmoid(o.astype(jnp.float32)).reshape(bsz, n, ML_HEADS, ML_DV)
        m_out = (hn * og).reshape(bsz, n, ML_HEADS * ML_DV).astype(o.dtype)
        c_out = gb * short_conv(gc * u, conv_w)
        return jnp.concatenate([m_out, c_out], axis=-1) @ w_out

    qkv_c, fwd_c, bwd_c, side_c = project(hc)
    qkv_x, fwd_x, bwd_x, side_x = project(hx)
    bsz = hx.shape[0]
    zero = (jnp.zeros((bsz, ML_HEADS, ML_DV, ML_DK), jnp.float32),
            jnp.zeros((bsz, ML_HEADS, ML_DK), jnp.float32),
            jnp.zeros((bsz, ML_HEADS), jnp.float32))
    h_cf, s_f = mlstm_direction(*qkv_c, *fwd_c, zero, False, with_ctx)
    h_cb, s_b = mlstm_direction(*qkv_c, *bwd_c, zero, True, with_ctx)
    h_xf, _ = mlstm_direction(*qkv_x, *fwd_x, s_f, False, True)
    h_xb, _ = mlstm_direction(*qkv_x, *bwd_x, s_b, True, True)
    y_x = combine(h_xf + h_xb, side_x)
    y_c = combine(h_cf + h_cb, side_c) if with_ctx else None
    return y_c, y_x

def gqa_attend(q, k, v):
    bsz, nq, _, _ = q.shape
    qg = q.reshape(bsz, nq, KV_HEADS, ATT_HEADS // KV_HEADS, HEAD_DIM)
    s = jnp.einsum('bqhgd,bkhd->bhgqk', qg, k).astype(jnp.float32) * HEAD_DIM ** -0.5
    p = jax.nn.softmax(s, axis=-1).astype(v.dtype)
    o = jnp.einsum('bhgqk,bkhd->bqhgd', p, v)
    return o.reshape(bsz, nq, ATT_HEADS * HEAD_DIM)

def attention_mixer(hc, hx, w_in, q_g, k_g, w_out, cos, sin, with_ctx):
    bsz, n, _ = hx.shape
    nq = ATT_HEADS * HEAD_DIM
    heads = lambda p, nh: p.reshape(bsz, p.shape[1], nh, HEAD_DIM)

    def kv(p):
        k, v = jnp.split(p, 2, axis=-1)
        return rms_norm(heads(k, KV_HEADS), k_g), heads(v, KV_HEADS)

    px = hx @ w_in
    qx = apply_axial_rope(rms_norm(heads(px[..., :nq], ATT_HEADS), q_g), cos, sin)
    kx, vx = kv(px[..., nq:])
    kx = apply_axial_rope(kx, cos, sin)
    if with_ctx:
        pc = hc @ w_in
        qc = rms_norm(heads(pc[..., :nq], ATT_HEADS), q_g)
        kc, vc = kv(pc[..., nq:])
    else:
        kc, vc = kv(hc @ w_in[:, nq:])
    k_all = jnp.concatenate([kc, kx], axis=1)
    v_all = jnp.concatenate([vc, vx], axis=1)
    nb = n // Q_BLOCK
    q_blocks = qx.reshape(bsz, nb, Q_BLOCK, ATT_HEADS, HEAD_DIM).swapaxes(0, 1)
    o_x = lax.map(lambda qb: gqa_attend(qb, k_all, v_all), q_blocks)
    y_x = o_x.swapaxes(0, 1).reshape(bsz, n, nq) @ w_out
    y_c = gqa_attend(qc, kc, vc) @ w_out if with_ctx else None
    return y_c, y_x

def first_inputs(seed: int = 0) -> dict:
    key = jax.random.key(seed)
    ks = jax.random.split(key, 20)
    nrm = lambda k, shape, s: jax.random.normal(k, shape, jnp.float32) * s
    d = D_MODEL
    ig_b = nrm(ks[11], (N_EVEN, 2, ML_HEADS), 0.1)
    fg_b = jnp.linspace(3.0, 6.0, ML_HEADS, dtype=jnp.float32)[None, None, :] + nrm(ks[12], (N_EVEN, 2, ML_HEADS), 0.1)
    return {
        "x": nrm(ks[0], (BATCH, SEQ, d), 1.0),
        "c": nrm(ks[1], (BATCH, d), 1.0),
        "ctx": nrm(ks[2], (BATCH, CTX_LEN, d), 1.0),
        "c_ctx": nrm(ks[3], (d,), 1.0),
        "ada_w": nrm(ks[4], (DEPTH, d, 6 * d), d ** -0.5),
        "ada_b": nrm(ks[5], (DEPTH, 6 * d), 0.02),
        "norm1_g": 1.0 + nrm(ks[6], (DEPTH, d), 0.05),
        "norm2_g": 1.0 + nrm(ks[7], (DEPTH, d), 0.05),
        "mlp_w1": nrm(ks[8], (DEPTH, d, MLP_HIDDEN), d ** -0.5),
        "mlp_w2": nrm(ks[9], (DEPTH, MLP_HIDDEN, d), MLP_HIDDEN ** -0.5),
        "hyb_w_in": nrm(ks[10], (N_EVEN, d, HYB_IN), d ** -0.5),
        "hyb_gate_b": jnp.stack([ig_b, fg_b], axis=2).reshape(N_EVEN, 4 * ML_HEADS),
        "mlstm_norm_g": 1.0 + nrm(ks[13], (N_EVEN, ML_HEADS * ML_DV), 0.05),
        "conv_w": nrm(ks[14], (N_EVEN, CONV_K, SC_WIDTH), CONV_K ** -0.5),
        "hyb_w_out": nrm(ks[15], (N_EVEN, HYB_OUT, d), HYB_OUT ** -0.5),
        "att_w_in": nrm(ks[16], (N_ODD, d, ATT_IN), d ** -0.5),
        "q_norm_g": 1.0 + nrm(ks[17], (N_ODD, HEAD_DIM), 0.05),
        "k_norm_g": 1.0 + nrm(ks[18], (N_ODD, HEAD_DIM), 0.05),
        "att_w_out": nrm(ks[19], (N_ODD, ATT_HEADS * HEAD_DIM, d), (ATT_HEADS * HEAD_DIM) ** -0.5),
    }

def first_block(x, c, ctx, c_ctx, ada_w, ada_b, norm1_g, norm2_g, mlp_w1, mlp_w2, hyb_w_in, hyb_gate_b,
              mlstm_norm_g, conv_w, hyb_w_out, att_w_in, q_norm_g, k_norm_g, att_w_out):
    rows = x.shape[1] // GRID_W
    cos, sin = axial_rope_tables(rows)
    silu_c = jax.nn.silu(c)
    silu_cc = jax.nn.silu(c_ctx)
    s_c = ctx
    for layer in range(DEPTH):
        last = layer == DEPTH - 1
        mod_x = jnp.split((silu_c @ ada_w[layer] + ada_b[layer])[:, None, :], 6, axis=-1)
        mod_c = jnp.split((silu_cc @ ada_w[layer] + ada_b[layer])[None, None, :], 6, axis=-1)
        hx = rms_norm(x, norm1_g[layer]) * (1 + mod_x[1]) + mod_x[0]
        hc = rms_norm(s_c, norm1_g[layer]) * (1 + mod_c[1]) + mod_c[0]
        if layer % 2 == 0:
            e = layer // 2
            y_c, y_x = hybrid_mixer(hc, hx, hyb_w_in[e], hyb_gate_b[e], mlstm_norm_g[e], conv_w[e], hyb_w_out[e], not last)
        else:
            o = layer // 2
            y_c, y_x = attention_mixer(hc, hx, att_w_in[o], q_norm_g[o], k_norm_g[o], att_w_out[o], cos, sin, not last)
        x = x + mod_x[2] * y_x
        x = x + mod_x[5] * sqrelu_mlp(rms_norm(x, norm2_g[layer]) * (1 + mod_x[4]) + mod_x[3], mlp_w1[layer], mlp_w2[layer])
        if not last:
            s_c = s_c + mod_c[2] * y_c
            s_c = s_c + mod_c[5] * sqrelu_mlp(rms_norm(s_c, norm2_g[layer]) * (1 + mod_c[4]) + mod_c[3], mlp_w1[layer], mlp_w2[layer])
    return x


D_MIX = D_MODEL
D_POOL = D_MIX // 2
D_SGU = D_MIX // 2
POOL_WINDOWS = (2, 4, 8, 16)
N_POOL_GROUPS = len(POOL_WINDOWS)
POOL_GROUP_DIM = D_POOL // N_POOL_GROUPS
CHUNK = 128
SGU_HEADS = 4
SGU_HEAD_DIM = D_SGU // SGU_HEADS
D_IN = D_POOL + 2 * D_SGU
D_FF = 2816
CONV_WIDTH = 3
N_MOD = 6
DEEPNORM_ALPHA = (2.0 * DEPTH) ** 0.25
DEEPNORM_BETA = (8.0 * DEPTH) ** -0.25
LN_EPS = 1e-5


def _layernorm(x, g, b):
    xf = x.astype(jnp.float32)
    mu = jnp.mean(xf, axis=-1, keepdims=True)
    var = jnp.mean(jnp.square(xf - mu), axis=-1, keepdims=True)
    y = (xf - mu) * lax.rsqrt(var + LN_EPS)
    return (y * g.astype(jnp.float32) + b.astype(jnp.float32)).astype(x.dtype)

def _modulate(x, shift, scale):
    return x * (1.0 + scale[:, None, :]) + shift[:, None, :]

def _pool_mixer(a, pool_w, pool_scale):
    B, S, _ = a.shape
    ag = a.reshape(B, S, N_POOL_GROUPS, POOL_GROUP_DIM).astype(jnp.float32)
    cs = jnp.cumsum(ag, axis=1)
    t = jnp.arange(S)
    pooled = []
    for g, w in enumerate(POOL_WINDOWS):
        csg = cs[:, :, g]
        prev = jnp.pad(csg, ((0, 0), (w, 0), (0, 0)))[:, :S]
        cnt = jnp.minimum(t + 1, w).astype(jnp.float32)[None, :, None]
        pooled.append((csg - prev) / cnt)
    pooled = (jnp.stack(pooled, axis=2) - ag).astype(a.dtype)
    mixed = jnp.einsum('bsgc,gcd->bsgd', pooled, pool_w)
    return mixed.reshape(B, S, D_POOL) * pool_scale

def _sgu_mixer(u, v, ln_g, ln_b, sgu_w, sgu_b):
    B, S, _ = v.shape
    u = jax.nn.gelu(u)
    v = _layernorm(jax.nn.gelu(v), ln_g, ln_b)
    vc = v.reshape(B, S // CHUNK, CHUNK, SGU_HEADS, SGU_HEAD_DIM)
    mask = jnp.tril(jnp.ones((CHUNK, CHUNK), dtype=bool))
    w = jnp.where(mask[None], sgu_w, jnp.zeros((), sgu_w.dtype))
    z = jnp.einsum('hts,bcshd->bcthd', w, vc) + jnp.transpose(sgu_b)[None, None, :, :, None]
    return u * z.reshape(B, S, D_SGU)

def _causal_dwconv(h, w, b):
    S = h.shape[1]
    hp = jnp.pad(h, ((0, 0), (CONV_WIDTH - 1, 0), (0, 0)))
    y = b
    for k in range(CONV_WIDTH):
        y = y + hp[:, k:k + S] * w[k]
    return y

def second_inputs(seed: int = 0) -> dict:
    key = jax.random.key(seed)
    ks = jax.random.split(key, 24)
    nrm = lambda k, shp: jax.random.normal(k, shp, dtype=jnp.float32)
    L, D = DEPTH, D_MODEL
    ada_b = jnp.concatenate([
        0.02 * nrm(ks[3], (L, 2 * D)),
        1.0 + 0.02 * nrm(ks[4], (L, D)),
        0.02 * nrm(ks[5], (L, 2 * D)),
        1.0 + 0.02 * nrm(ks[6], (L, D)),
    ], axis=-1)
    return {
        "x": nrm(ks[0], (BATCH, SEQ, D)),
        "c": nrm(ks[1], (BATCH, D)),
        "ada_w": 0.1 * D ** -0.5 * nrm(ks[2], (L, D, N_MOD * D)),
        "ada_b": ada_b,
        "w_in": D ** -0.5 * nrm(ks[7], (L, D, D_IN)),
        "pool_w": POOL_GROUP_DIM ** -0.5 * nrm(ks[8], (L, N_POOL_GROUPS, POOL_GROUP_DIM, POOL_GROUP_DIM)),
        "pool_scale": 1.0 + 0.02 * nrm(ks[9], (L, D_POOL)),
        "sgu_ln_g": 1.0 + 0.02 * nrm(ks[10], (L, D_SGU)),
        "sgu_ln_b": 0.02 * nrm(ks[11], (L, D_SGU)),
        "sgu_w": CHUNK ** -0.5 * nrm(ks[12], (L, SGU_HEADS, CHUNK, CHUNK)),
        "sgu_b": 1.0 + 0.02 * nrm(ks[13], (L, SGU_HEADS, CHUNK)),
        "w_out": DEEPNORM_BETA * D_MIX ** -0.5 * nrm(ks[14], (L, D_MIX, D)),
        "ln1_g": 1.0 + 0.02 * nrm(ks[15], (L, D)),
        "ln1_b": 0.02 * nrm(ks[16], (L, D)),
        "w_up": D ** -0.5 * nrm(ks[17], (L, D, 2 * D_FF)),
        "conv_w": 0.5 * nrm(ks[18], (L, CONV_WIDTH, D_FF)),
        "conv_b": 0.02 * nrm(ks[19], (L, D_FF)),
        "w_down": DEEPNORM_BETA * D_FF ** -0.5 * nrm(ks[20], (L, D_FF, D)),
        "ln2_g": 1.0 + 0.02 * nrm(ks[21], (L, D)),
        "ln2_b": 0.02 * nrm(ks[22], (L, D)),
    }

def second_block(x, c, ada_w, ada_b, w_in, pool_w, pool_scale, sgu_ln_g, sgu_ln_b, sgu_w, sgu_b,
              w_out, ln1_g, ln1_b, w_up, conv_w, conv_b, w_down, ln2_g, ln2_b):
    c_act = jax.nn.silu(c)
    for l in range(DEPTH):
        mod = c_act @ ada_w[l] + ada_b[l]
        shift1, scale1, gate1, shift2, scale2, gate2 = jnp.split(mod, N_MOD, axis=-1)

        h = _modulate(x, shift1, scale1)
        proj = jnp.einsum('bsd,de->bse', h, w_in[l])
        a = proj[..., :D_POOL]
        u = proj[..., D_POOL:D_POOL + D_SGU]
        v = proj[..., D_POOL + D_SGU:]
        y_a = _pool_mixer(a, pool_w[l], pool_scale[l])
        y_b = _sgu_mixer(u, v, sgu_ln_g[l], sgu_ln_b[l], sgu_w[l], sgu_b[l])
        mix = jnp.concatenate([y_a, y_b], axis=-1)
        f = jnp.einsum('bse,ed->bsd', mix, w_out[l])
        x = _layernorm(DEEPNORM_ALPHA * x + gate1[:, None, :] * f, ln1_g[l], ln1_b[l])

        h = _modulate(x, shift2, scale2)
        up = jnp.einsum('bsd,df->bsf', h, w_up[l])
        g, val = up[..., :D_FF], up[..., D_FF:]
        g = _causal_dwconv(g, conv_w[l], conv_b[l])
        f = jnp.einsum('bsf,fd->bsd', jax.nn.gelu(g) * val, w_down[l])
        x = _layernorm(DEEPNORM_ALPHA * x + gate2[:, None, :] * f, ln2_g[l], ln2_b[l])
    return x


_first_inputs = second_inputs


def second_inputs(seed=0):
    import zlib

    import numpy as np

    out = dict(_first_inputs(seed))
    spreads = {}
    factors = {'pool_scale': 8.0, 'sgu_ln_g': 8.0, 'sgu_ln_b': 8.0, 'sgu_b': 8.0, 'conv_b': 8.0}
    for name, (base, spread) in spreads.items():
        noise = np.random.default_rng([zlib.crc32(name.encode()), seed]).standard_normal(out[name].shape)
        drawn = base * np.exp(spread * noise) if base else spread * noise
        out[name] = __import__('jax').numpy.asarray(drawn.astype(out[name].dtype))
    for name, factor in factors.items():
        out[name] = (out[name] * factor).astype(out[name].dtype)
    return out


_narrow_inputs = second_inputs


def second_inputs(seed=0):

    out = dict(_narrow_inputs(seed))
    wider = {'pool_scale': 3.06, 'sgu_ln_g': 6.07, 'sgu_ln_b': 5.86, 'sgu_b': 4.07}
    for name, times in wider.items():
        mean = out[name].mean()
        out[name] = (mean + times * (out[name] - mean)).astype(out[name].dtype)
    return out


def setup_inputs(seed=0):
    out = dict(first_inputs(seed))
    for name, value in second_inputs(seed + 1).items():
        if name != "x":
            out[name + "_2"] = value
    return out


def reference(
    x, c, ctx, c_ctx, ada_w, ada_b, norm1_g, norm2_g, mlp_w1, mlp_w2, hyb_w_in, hyb_gate_b,
    mlstm_norm_g, conv_w, hyb_w_out, att_w_in, q_norm_g, k_norm_g, att_w_out, c_2, ada_w_2,
    ada_b_2, w_in_2, pool_w_2, pool_scale_2, sgu_ln_g_2, sgu_ln_b_2, sgu_w_2, sgu_b_2, w_out_2,
    ln1_g_2, ln1_b_2, w_up_2, conv_w_2, conv_b_2, w_down_2, ln2_g_2, ln2_b_2,
):
    x = first_block(
        x, c, ctx, c_ctx, ada_w, ada_b, norm1_g, norm2_g, mlp_w1, mlp_w2, hyb_w_in, hyb_gate_b,
        mlstm_norm_g, conv_w, hyb_w_out, att_w_in, q_norm_g, k_norm_g, att_w_out,
    )
    return second_block(
        x, c_2, ada_w_2, ada_b_2, w_in_2, pool_w_2, pool_scale_2, sgu_ln_g_2, sgu_ln_b_2,
        sgu_w_2, sgu_b_2, w_out_2, ln1_g_2, ln1_b_2, w_up_2, conv_w_2, conv_b_2, w_down_2,
        ln2_g_2, ln2_b_2,
    )


_drawn_inputs = setup_inputs


def setup_inputs(seed=0):
    import zlib

    import numpy as np

    out = dict(_drawn_inputs(seed))
    spreads = {}
    factors = {'mlstm_norm_g': 4.865, 'q_norm_g': 8.0, 'k_norm_g': 8.0}
    for name, (base, spread) in spreads.items():
        noise = np.random.default_rng([zlib.crc32(name.encode()), seed]).standard_normal(out[name].shape)
        drawn = base * np.exp(spread * noise) if base else spread * noise
        out[name] = __import__('jax').numpy.asarray(drawn.astype(out[name].dtype))
    for name, factor in factors.items():
        out[name] = (out[name] * factor).astype(out[name].dtype)
    return out
```

```python
from contextlib import ExitStack

import numpy as np

import concourse.bass as bass
from concourse import mybir

ALU = mybir.AluOpType
ACT = mybir.ActivationFunctionType
AX = mybir.AxisListType
F32 = mybir.dt.float32
F32R = mybir.dt.float32r

P = 128
D = 1024
KD = D // P
NC, NX = 256, 512
NT = NC + NX
TT = NT // P
MH, DK, DV = 4, 64, 128
SCW = 512
HID = 4096
AH, KVH, HD = 16, 4, 64
FF = 2816
SGH = 4
GRID_W = 64
POOL_W = (2, 4, 8, 16)
EPS, LN_EPS = 1e-6, 1e-5
ALPHA = (2.0 * 2) ** 0.25
BIG = 1e30
GW = 36
PADW = NT + 4

N_HYB, N_OUT, N_MLP, N_ATT, N_MIX = 25, 8, 64, 12, 12
CH = 8
T_HYB = 0
T_HOUT = T_HYB + N_HYB
T_MLP0 = T_HOUT + N_OUT
T_ATT = T_MLP0 + N_MLP
T_AOUT = T_ATT + N_ATT
T_MLP1 = T_AOUT + N_OUT
T_S = T_MLP1 + N_MLP
NF = FF // P
N_FF = 2 * NF + 3 * KD
N_S = N_MIX + N_OUT + N_FF
N_UNITS = T_S + 2 * N_S
ADA = 48

_at = {}
_n = 0
for _name, _w in (("ada_b", 4 * ADA), ("norm1_g", 16), ("norm2_g", 16), ("gate_b", 1), ("mnorm_g", 4),
                  ("conv_w", 12), ("q_g", 1), ("k_g", 1), ("pool_scale", 8), ("ln1_g", 16), ("ln1_b", 16),
                  ("ln2_g", 16), ("ln2_b", 16), ("ff_conv_w", 2 * 3 * NF), ("ff_conv_b", 2 * NF),
                  ("eps", 1), ("ln_eps", 1)):
    _at[_name] = _n
    _n += _w
VEC_AT, VEC_N = dict(_at), _n
C_ID, C_ONE, C_BD, C_ROT, C_MF, C_MB, C_TRI, C_RC = [P * i for i in range(8)]
CON_N = 7 * P + 64


class At:

    def __init__(self, c, i=None, s=0):
        self.c, self.i, self.s = c, i, s

    def __add__(self, n):
        return At(self.c + n, self.i, self.s)

    def __mod__(self, n):
        assert self.i is None or self.s % n == 0
        return self.c % n

    def __floordiv__(self, n):
        assert self.i is None or self.s % n == 0
        return At(self.c // n, self.i, self.s // n)

    def times(self, n):
        return At(self.c * n, self.i, self.s * n)

    def value(self):
        return self.c if self.i is None else self.i * self.s + self.c

    def positive(self):
        assert self.i is None or self.c > 0, "a loop's first wait would be for nothing"
        return self.c > 0


def wait(eng, sem, at):
    if not isinstance(at, At):
        at = At(at)
    if at.positive():
        eng.wait_ge(sem, at.value())


def build(nc, xin, cvec, wstream, adaw, vecs_d, consts_d, rope_d, poolw_d, sguw_d, rows_d, out):
    ctx = ExitStack()
    with ctx:
        def sb(name, shape, dt=F32, where=ctx):
            return where.enter_context(nc.sbuf_tensor(name, shape, dt))

        def sem(name):
            return ctx.enter_context(nc.semaphore(name))

        X = sb("X", [P, KD, NT])
        Wraw = sb("Wraw", [P, 4, D])
        Whi = sb("Whi", [P, 2, D], F32R)
        Wlo = sb("Wlo", [P, 2, D], F32R)
        Araw = sb("Araw", [P, 2, D])
        CB = sb("CB", [P, 2, D])
        VEC = sb("VEC", [P, VEC_N])
        CON = sb("CON", [P, CON_N])
        Junk = sb("Junk", [P, D])
        MOD = sb("MOD", [P, 2, 2, ADA])
        MRAW = sb("MRAW", [P, 2, 2, ADA])
        GAIN = sb("GAIN", [P, 2, 2, 2, KD])
        OFFS = sb("OFFS", [P, 2, KD])
        LNA = sb("LNA", [P, 4, KD])
        SQ = sb("SQ", [P, 2, NT])
        T = sb("T", [P, 2, PADW])
        RS = sb("RS", [P, NT])
        ACOL = sb("ACOL", [P, TT, GW])
        small = sb("small", [P, 64])
        ident = CON[:, C_ID:C_ID + P]
        ones = CON[:, C_ONE:C_ONE + P]
        blockones = CON[:, C_BD:C_BD + P]
        rotate = CON[:, C_ROT:C_ROT + P]
        mask_f = CON[:, C_MF:C_MF + P]
        mask_b = CON[:, C_MB:C_MB + P]
        tri = CON[:, C_TRI:C_TRI + P]

        hyb = ExitStack()
        HQ = sb("HQ", [P, 2, NT], where=hyb)
        HK = sb("HK", [P, 2, NT], where=hyb)
        HV = sb("HV", [P, TT, MH * DV], where=hyb)
        SO = sb("SO", [P, MH, NT], where=hyb)
        CY = sb("CY", [P, 4, 772], where=hyb)
        RM = sb("RM", [P, NT], where=hyb)
        p1 = ExitStack()
        h0 = [sb("h0_hi", [P, KD, NT], F32R, p1), sb("h0_lo", [P, KD, NT], F32R, p1)]
        rows = [sb(f"rows{i}", [P, NT], where=p1) for i in range(3)]
        p1.close()
        p2 = ExitStack()
        mixa = [sb("mixa_hi", [P, 4, NT], F32R, p2), sb("mixa_lo", [P, 4, NT], F32R, p2)]
        Mb = sb("Mb", [P, NT], where=p2)
        MD = sb("MD", [P, NT], where=p2)
        HF = sb("HF", [P, NT], where=p2)
        p3 = ExitStack()
        PW = sum(NT - P * i for i in range(TT))
        PB = sb("PB", [P, 2, PW], where=p3)
        p3.close()
        mixb = [sb("mixb_hi", [P, 4, NT], F32R, p2), sb("mixb_lo", [P, 4, NT], F32R, p2)]
        p2.close()
        hyb.close()

        p4 = ExitStack()
        h1 = [sb("h1_hi", [P, KD, NT], F32R, p4), sb("h1_lo", [P, KD, NT], F32R, p4)]
        hid0 = [sb("hid0_hi", [P, CH, NT], F32R, p4), sb("hid0_lo", [P, CH, NT], F32R, p4)]
        p4.close()

        att = ExitStack()
        AQ = sb("AQ", [P, 8, NX], where=att)
        AK = sb("AK", [P, 2, NT], where=att)
        AV = sb("AV", [P, TT, KVH * HD], where=att)
        p5 = ExitStack()
        h2 = [sb("h2_hi", [P, KD, NT], F32R, p5), sb("h2_lo", [P, KD, NT], F32R, p5)]
        ROPE = sb("ROPE", [P, 2, NX], where=p5)
        QN = sb("QN", [P, 2, NT], where=p5)
        RT = sb("RT", [P, NX], where=p5)
        p5.close()
        p6 = ExitStack()
        ao = [sb("ao_hi", [P, KD, NX], F32R, p6), sb("ao_lo", [P, KD, NX], F32R, p6)]
        PR = sb("PR", [P, 2, NT], where=p6)
        PT = sb("PT", [P, 2, TT, NX], where=p6)
        NM = sb("NM", [P, 64], where=p6)
        ZS = sb("ZS", [P, 64], where=p6)
        ZR = sb("ZR", [P, 64], where=p6)
        p6.close()
        att.close()

        p7 = ExitStack()
        h3 = [sb("h3_hi", [P, KD, NX], F32R, p7), sb("h3_lo", [P, KD, NX], F32R, p7)]
        hid1 = [sb("hid1_hi", [P, CH, NX], F32R, p7), sb("hid1_lo", [P, CH, NX], F32R, p7)]
        p7.close()

        p8 = ExitStack()
        hs = [sb("hs_hi", [P, KD, NX], F32R, p8), sb("hs_lo", [P, KD, NX], F32R, p8)]
        p9 = ExitStack()
        ms = [sb("ms_hi", [P, KD, NX], F32R, p9), sb("ms_lo", [P, KD, NX], F32R, p9)]
        PAD = 16
        PA = sb("PA", [P, SGH, PAD + NX], where=p9)
        PS = sb("PS", [P, 2, PAD + NX], where=p9)
        PO = sb("PO", [P, NX], where=p9)
        UG = sb("UG", [P, SGH, NX], where=p9)
        VT = sb("VT", [P, 4, NX], where=p9)
        SW = sb("SW", [P, SGH, P], where=p9)
        POW = sb("POW", [P, SGH, P], where=p9)
        ROW = sb("ROW", [P, 3, NX], where=p9)
        p9.close()
        hid2 = [sb("hid2_hi", [P, CH, NX], F32R, p8), sb("hid2_lo", [P, CH, NX], F32R, p8)]
        GP = sb("GP", [P, 2, 2 + NX], where=p8)
        CV = sb("CV", [P, 2, NX], where=p8)
        p8.close()

        G = [ctx.enter_context(nc.psum_tensor(f"G{i}", [P, 1024], F32)) for i in range(2)]
        B4 = ctx.enter_context(nc.psum_tensor("B4", [P, 1024], F32))
        B6 = ctx.enter_context(nc.psum_tensor("B6", [P, 1024], F32))

        def ps(bank, a, b):
            return bank[:, NC + a:NC + b]

        w_raw = [sem(f"w_raw{i}") for i in range(4)]
        ada_raw = [sem(f"ada_raw{i}") for i in range(2)]
        x_in, c_in, small_in, late_in, out_dma = map(sem, ("x_in", "c_in", "small_in", "late_in", "out_dma"))
        w_hi, w_lo, tile_done = map(sem, ("w_hi", "w_lo", "tile_done"))
        tile_free = [sem(f"tile_free{i}") for i in range(2)]
        ada_used, silu_done, silu_ready = map(sem, ("ada_used", "silu_done", "silu_ready"))
        cb_free, mods, vlink = map(sem, ("cb_free", "mods", "vlink"))
        src_ready, hid_ready = map(sem, ("src_ready", "hid_ready"))
        sq_ready, sq_used, std_ready, rstd_ready, nt_ready, nhi_ready = map(
            sem, ("sq_ready", "sq_used", "std_ready", "rstd_ready", "nt_ready", "nhi_ready"))
        stat_done = sem("stat_done")
        gate_step, turned, turn_used = map(sem, ("gate_step", "turned", "turn_used"))
        cu_done, acol_ps, acol_ready = map(sem, ("cu_done", "acol_ps", "acol_ready"))
        m_ps, m_used, md_ready, d_ready, sc_done, p_ready, pv_done, nd_used, em_ready = map(
            sem, ("m_ps", "m_used", "md_ready", "d_ready", "sc_done", "p_ready", "pv_done", "nd_used", "em_ready"))
        hsum_ready, hsq_ready, hstat_done, hstd_ready, ht_ready, hhi_ready = map(
            sem, ("hsum_ready", "hsq_ready", "hstat_done", "hstd_ready", "ht_ready", "hhi_ready"))
        hsq2_ready, hidhi_ready = map(sem, ("hsq2_ready", "hidhi_ready"))
        qk_sq, qk_stat, qk_std, qk_n, rot_done, qk_ready = map(
            sem, ("qk_sq", "qk_stat", "qk_std", "qk_n", "rot_done", "qk_ready"))
        as_done, amax_ready, aexp_done, aprob_ready, at_done, at_used, apv_done, ao_hi_ready = map(
            sem, ("as_done", "amax_ready", "aexp_done", "aprob_ready", "at_done", "at_used", "apv_done",
                  "ao_hi_ready"))
        mean_done, centred, ln_hi_ready, ln_x_ready, ln_t_ready = map(
            sem, ("mean_done", "centred", "ln_hi_ready", "ln_x_ready", "ln_t_ready"))
        pooled, pool_done, v_turned, v_turn_used = map(sem, ("pooled", "pool_done", "v_turned", "v_turn_used"))
        v_var, v_std, v_normed, tri_ready, gated_ps, gated_ready, mix_hi = map(
            sem, ("v_var", "v_std", "v_normed", "tri_ready", "gated_ps", "gated_ready", "mix_hi"))
        ffconv0, ffconv, ffgelu, ffhi = map(sem, ("ffconv0", "ffconv", "ffgelu", "ffhi"))

        FULL, LAT = (0, NT), (NC, NT)

        def parts(rng):
            return [(0, NC), (NC, NT)] if rng == FULL else [(NC, NT)]

        S_N0, S_MIX, S_N1, S_N2, S_AO, S_N3 = range(6)

        def s_set(l, what):
            return 6 + 3 * l + what

        def freed(eng, t):
            wait(eng, tile_free[t % 2], t // 2 + 1)

        H_M0, H_M1 = 0, 32
        def h_s(l):
            return 64 + NF * l

        block = ctx.enter_context(nc.Block())

        @block.sync
        def _(sp):
            sp.dma_start(X[:, 0:4, :], xin[:, 0:4, :]).then_inc(x_in, 16)
            sp.dma_start(VEC[:, :], vecs_d).then_inc(small_in, 16)
            sp.dma_start(CON[:, :], consts_d).then_inc(small_in, 16)
            sp.dma_start(X[:, 4:8, :], xin[:, 4:8, :]).then_inc(x_in, 16)

            def load(t):
                wait(sp, w_lo, t + -3)
                s = t % 4
                sp.dma_start(Wraw[:, s, :], wstream[bass.ds(t.value(), 1), :, :].rearrange("a p n -> p (a n)")
                             if t.i is not None else wstream[t.c]).then_inc(w_raw[s], 16)

            def stream(a, b):
                n = (b - a) // 4
                if n > 1:
                    with sp.Fori(0, n) as i:
                        for j in range(4):
                            load(At(a + j, i, 4))
                for u in range(a + (4 * n if n > 1 else 0), b):
                    load(At(u))

            for u in range(4):
                load(At(u))
            stream(4, T_ATT + 4)
            sp.wait_ge(src_ready, 8 * S_N2 + 1)
            sp.dma_start(ROPE[:, :, :], rope_d).then_inc(late_in, 16)
            stream(T_ATT + 4, T_S)
            for l in range(2):
                t0 = T_S + l * N_S
                stream(t0, t0 + 4)
                sp.wait_ge(src_ready, 8 * s_set(l, 0) + 8)
                sp.dma_start(POW[:, :, :], poolw_d[l]).then_inc(late_in, 16)
                sp.dma_start(SW[:, :, :], sguw_d[l]).then_inc(late_in, 16)
                sp.dma_start(ROW[:, :, :], rows_d[l]).then_inc(late_in, 16)
                stream(t0 + 4, t0 + N_S)
            for k in range(KD):
                sp.wait_ge(ln_x_ready, 8 * 3 + k + 1)
                sp.dma_start(out[:, k, :], X[:, k, NC:NT]).then_inc(out_dma, 16)
            sp.wait_ge(out_dma, 16 * KD)

        @block.gpsimd
        def _(pool):
            pool.dma_start(CB[:, 0, :], cvec[0]).then_inc(c_in, 16)
            pool.dma_start(CB[:, 1, :], cvec[1]).then_inc(c_in, 16)

            def load(n):
                wait(pool, ada_used, n + -1)
                pool.dma_start(Araw[:, n % 2, :], adaw[bass.ds(n.value(), 1), :, :].rearrange("a p n -> p (a n)")
                               if n.i is not None else adaw[n.c]).then_inc(ada_raw[n % 2], 16)

            for n in range(2):
                load(At(n))
            with pool.Fori(0, (2 * ADA - 2) // 2) as i:
                for j in range(2):
                    load(At(2 + j, i, 2))
            pool.wait_ge(cb_free, 1)
            pool.dma_start(CB[:, 0, :], cvec[2]).then_inc(c_in, 16)
            with pool.Fori(0, ADA) as i:
                for j in range(2):
                    load(At(2 * ADA + j, i, 2))

        @block.tensor
        def _(pe):
            def product(t, src, rng, kt=KD, ready=None):
                wait(pe, w_lo, t + 1)
                wait(pe, tile_free[t % 2], t // 2)
                s = t % 2
                for n, (a, b) in enumerate(parts(rng)):
                    for k in range(kt):
                        if ready is not None and n == 0:
                            pe.wait_ge(ready[0], (ready[1] + (k + 1)).value())
                        hi, lo = src(k)
                        wh, wl = Whi[:, s, k * P:(k + 1) * P], Wlo[:, s, k * P:(k + 1) * P]
                        o = ps(G[s], a, b)
                        pe.matmul(o, wh, hi[:, a:b], start=(k == 0), stop=False)
                        pe.matmul(o, wh, lo[:, a:b], start=False, stop=False)
                        last = pe.matmul(o, wl, hi[:, a:b], start=False, stop=(k == kt - 1))
                last.then_inc(tile_done, 1)

            def tiles(pair):
                return lambda k: (pair[0][:, k, :], pair[1][:, k, :])

            def latent(pair):
                class Shifted:
                    def __init__(self, ap):
                        self.ap = ap

                    def __getitem__(self, key):
                        return self.ap[:, key[1].start - NC:key[1].stop - NC]

                return lambda k: (Shifted(pair[0][:, k, :]), Shifted(pair[1][:, k, :]))

            def norm_stats(n, rng):
                for k in range(KD):
                    pe.wait_ge(sq_ready, 8 * n + k + 1)
                    for a, b in parts(rng):
                        last = pe.matmul(ps(B4, a, b), ones, SQ[:, k % 2, a:b], start=(k == 0), stop=(k == KD - 1))
                    last.then_inc(sq_used, 1)

            def turn(n, first, count):
                freed(pe, At(5 + n if n < 4 else T_ATT + n - 4))
                wait(pe, turn_used, n)
                for i in range(count):
                    last = pe.transpose(B6[:, i * P:(i + 1) * P], T[:, n % 2, first + i * P:first + (i + 1) * P],
                                        ident)
                last.then_inc(turned, 1)

            def mlp(t0, h, hid, rng, sset, h0_):
                src = tiles(h) if rng == FULL else latent(h)
                hsrc = tiles(hid) if rng == FULL else latent(hid)

                def chunk(i, ready):
                    for j in range(CH):
                        product(At(t0 + j, i, 2 * CH), src, rng, ready=ready if j == 0 else None)
                    for m in range(KD):
                        product(At(t0 + CH + m, i, 2 * CH), hsrc, rng,
                                ready=(hid_ready, At(h0_, i, CH)) if m == 0 else None)

                with pe.Fori(0, HID // P // CH) as i:
                    chunk(i, (src_ready, At(8 * sset)))

            pe.wait_ge(small_in, 32)
            norm_stats(0, FULL)
            src = tiles(h0)
            product(At(0), src, FULL, ready=(src_ready, At(8 * S_N0)))
            for t in range(1, N_HYB):
                product(At(t), src, FULL)
                if 6 <= t < 10:
                    turn(t - 6, 0, TT)
            pe.wait_ge(gate_step, 15)
            for i in range(TT):
                last = pe.transpose(B4[:, i * GW:(i + 1) * GW], rows[1][0:GW, i * P:(i + 1) * P], ident[0:GW, 0:GW])
            last.then_inc(acol_ps, 1)
            def pieces(d):
                out_ = []
                order = (0, 1, 2, 3, 4, 5) if d == 0 else (1, 0, 5, 4, 3, 2)
                for i in order:
                    if i < 2:
                        out_.append((i, (P * i, NC) if d == 0 else (0, P * (i + 1))))
                        out_.append((i, (NC, NT)))
                    else:
                        out_.append((i, (P * i, NT) if d == 0 else (NC, P * (i + 1))))
                return out_

            def p_at(d):
                at, n = [], 0
                for _, (a, b) in pieces(d):
                    at.append(n)
                    n += b - a
                return at

            def spread(q, base, n):
                wait(pe, m_used, n)
                h, d = q // 2, q % 2
                sel = ident[base:base + GW, base + 32 * d + h:base + 32 * d + h + 1].to_broadcast([GW, P])
                for a, b in parts(FULL):
                    last = pe.matmul(ps(B4, a, b), sel, RM[base:base + GW, a:b], start=True, stop=True)
                last.then_inc(m_ps, 1)

            pe.wait_ge(acol_ready, 1)
            for q in range(2 * MH):
                h, d = q // 2, q % 2
                kb = DK * (h % 2)
                spread(q, 0, 2 * q)
                pc, at = pieces(d), p_at(d)
                if q == 0:
                    pe.wait_ge(tile_free[0], (N_HYB + 1) // 2)
                    pe.wait_ge(tile_free[1], N_HYB // 2)

                def weights(n):
                    i, (a, b) = pc[n]
                    r = 8 * q + n
                    wait(pe, p_ready, r - 1)
                    pe.matmul(G[0][:, 512 * (r % 2):512 * (r % 2) + b - a], HK[kb:kb + DK, h // 2, P * i:P * (i + 1)],
                              HQ[kb:kb + DK, h // 2, a:b], start=True, stop=True).then_inc(sc_done, 1)

                def values(n):
                    i, (a, b) = pc[n]
                    r = 8 * q + n
                    pe.wait_ge(p_ready, r + 1)
                    if n == 0:
                        wait(pe, nd_used, q)
                    probs = PB[:, d, at[n]:at[n] + b - a]
                    pe.matmul(ps(B6, a, b), HV[:, i, h * DV:(h + 1) * DV], probs, start=n in (0, 1), stop=n in (2, 7),
                              skip_group_check=True)
                    return pe.matmul(ps(G[1], a, b), ones, probs, start=n in (0, 1), stop=n in (2, 7),
                                     skip_group_check=True)

                weights(0)
                for n in range(8):
                    if n < 7:
                        weights(n + 1)
                    last = values(n)
                last.then_inc(pv_done, 1)
                spread(q, 64, 2 * q + 1)
                if d == 1:
                    pe.wait_ge(hsq_ready, h + 1)
                    pe.wait_ge(m_used, 2 * q + 2)
                    for a, b in parts(FULL):
                        last = pe.matmul(ps(B4, a, b), ones, SQ[:, 0, a:b], start=True, stop=True)
                    last.then_inc(hstat_done, 1)
                    pe.wait_ge(hstd_ready, h + 1)
            def mixed(k):
                return (mixa[0][:, k, :], mixa[1][:, k, :]) if k < 4 else (mixb[0][:, k - 4, :], mixb[1][:, k - 4, :])

            pe.wait_ge(nd_used, 2 * MH)
            for m in range(KD):
                product(At(T_HOUT + m), mixed, FULL, ready=(src_ready, At(8 * S_MIX)) if m == 0 else None)
            norm_stats(1, FULL)
            mlp(T_MLP0, h1, hid0, FULL, S_N1, H_M0)
            norm_stats(2, FULL)
            src = tiles(h2)

            def qk_stats(n, rng):
                pe.wait_ge(qk_sq, n + 1)
                wait(pe, qk_std, n)
                for a, b in parts(rng):
                    last = pe.matmul(ps(B4, a, b), blockones, SQ[:, n % 2, a:b], start=True, stop=True)
                last.then_inc(qk_stat, 1)

            def qk_rotate(n):
                pe.wait_ge(qk_n, n + 1)
                wait(pe, qk_ready, n)
                if n == 0:
                    pe.wait_ge(turn_used, 6)
                pe.matmul(B6[:, 0:NX], rotate, QN[:, n % 2, NC:NT], start=True, stop=True).then_inc(rot_done, 1)

            for t in range(N_ATT):
                rng = FULL if t < 4 else LAT
                product(At(T_ATT + t), src, rng, ready=(src_ready, At(8 * S_N2)) if t == 0 else None)
                if 1 <= t < 3:
                    turn(4 + t - 1, 0, TT)
                if t >= 3:
                    qk_stats(t - 3, FULL if t - 3 < 2 else LAT)
                if t >= 4:
                    qk_rotate(t - 4)
            qk_stats(9, LAT)
            qk_rotate(8)
            qk_rotate(9)
            def score(it):
                j, b, qt = it // 8, it // 4 % 2, it % 4
                kb = HD * b
                if it == 0:
                    pe.wait_ge(qk_ready, 10)
                    pe.wait_ge(tile_free[0], (T_AOUT + 1) // 2)
                    pe.wait_ge(tile_free[1], T_AOUT // 2)
                wait(pe, aexp_done, it - 1)
                q = AQ[kb:kb + HD, j, qt * P:(qt + 1) * P]
                pe.matmul(G[it % 2][:, 0:512], q, AK[kb:kb + HD, j // 4, 0:512], start=True, stop=True)
                pe.matmul(G[it % 2][:, 512:NT], q, AK[kb:kb + HD, j // 4, 512:NT], start=True,
                          stop=True).then_inc(as_done, 1)

            def turn_probs(it):
                pe.wait_ge(aprob_ready, it + 1)
                wait(pe, at_used, it)
                for i in range(TT):
                    last = pe.transpose(B4[:, i * P:(i + 1) * P], PR[:, it % 2, i * P:(i + 1) * P], ident)
                last.then_inc(at_done, 1)

            def attend(hn):
                j, b = hn // 2, hn % 2
                g = 2 * (j // 4) + b
                pe.wait_ge(at_used, 4 * hn + 4)
                if b == 0:
                    wait(pe, src_ready, 8 * S_AO + j - 1 if j > 1 else 0)
                for i in range(TT):
                    last = pe.matmul(B6[HD * b:HD * (b + 1), 512 * (j % 2):512 * (j % 2) + NX],
                                     AV[:, i, g * HD:(g + 1) * HD], PT[:, hn % 2, i, :],
                                     start=(i == 0), stop=(i == TT - 1))
                last.then_inc(apv_done, 1)

            score(0)
            for it in range(4 * AH):
                if it + 1 < 4 * AH:
                    score(it + 1)
                turn_probs(it)
                if it % 4 == 0 and it > 0:
                    attend(it // 4 - 1)
            attend(AH - 1)
            pe.wait_ge(aexp_done, 4 * AH)
            src = latent(ao)
            for m in range(KD):
                product(At(T_AOUT + m), src, LAT, ready=(src_ready, At(8 * S_AO)) if m == 0 else None)
            norm_stats(3, LAT)
            mlp(T_MLP1, h3, hid1, LAT, S_N3, H_M1)
            def stream_at(n):
                return T_S + (n // 2) * N_S + N_MIX if n % 2 == 0 else T_S + (n // 2 + 1) * N_S - KD

            def ln_stats(n):
                for k in range(KD):
                    freed(pe, At(stream_at(n) + k))
                    last = pe.matmul(B4[:, 512:1024], ones, X[:, k, NC:NT], start=(k == 0), stop=(k == KD - 1))
                last.then_inc(mean_done, 1)
                for k in range(KD):
                    pe.wait_ge(sq_ready, 32 + 8 * n + k + 1)
                    if k == 0:
                        pe.wait_ge(centred, 8 * n + 8)
                    last = pe.matmul(B4[:, 512:1024], ones, SQ[:, k % 2, 0:NX], start=(k == 0), stop=(k == KD - 1))
                    last.then_inc(sq_used, 1)

            for l in range(2):
                t0 = T_S + l * N_S
                src = latent(hs)
                for t in range(N_MIX):
                    product(At(t0 + t), src, LAT, ready=(src_ready, At(8 * s_set(l, 0))) if t == 0 else None)
                    if 1 <= t < 5:
                        n = 4 * l + t - 1
                        freed(pe, At(t0 + t - 1))
                        wait(pe, v_turn_used, n)
                        for i in range(4):
                            last = pe.transpose(B6[:, i * P:(i + 1) * P], T[:, n % 2, i * P:(i + 1) * P], ident)
                        last.then_inc(v_turned, 1)
                for g in range(SGH):
                    n = 4 * l + g
                    pe.wait_ge(pooled, n + 1)
                    if g == 0:
                        pe.wait_ge(late_in, 16 + 48 * (l + 1))
                        pe.wait_ge(v_turn_used, 4 * l + 4)
                    if g >= 2:
                        pe.wait_ge(src_ready, 8 * s_set(l, 1) + g - 1)
                    pe.matmul(B6[:, 512 * (g % 2):512 * (g % 2) + NX], POW[:, g, :], PO[:, :], start=True,
                              stop=True).then_inc(pool_done, 1)
                pe.wait_ge(v_normed, l + 1)
                pe.wait_ge(tri_ready, l + 1)
                for h in range(SGH):
                    n = 4 * l + h
                    pe.wait_ge(src_ready, 8 * s_set(l, 1) + 4 + h - 1)
                    for c in range(4):
                        last = pe.matmul(B6[:, 512 * (h % 2) + c * P:512 * (h % 2) + (c + 1) * P],
                                         VT[:, c, h * P:(h + 1) * P], SW[:, h, :], start=True, stop=True)
                    last.then_inc(gated_ps, 1)
                src = latent(ms)
                for m in range(KD):
                    product(At(t0 + N_MIX + m), src, LAT,
                            ready=(src_ready, At(8 * s_set(l, 1))) if m == 0 else None)
                ln_stats(2 * l)
                t1 = t0 + N_MIX + N_OUT
                src, hsrc = latent(hs), latent(hid2)

                def chunk(i, c0, n_up):
                    for j in range(2 * n_up):
                        product(At(t1 + 24 * c0 + j, i, 24), src, LAT,
                                ready=(src_ready, At(8 * s_set(l, 2))) if j == 0 else None)
                    for m in range(KD):
                        product(At(t1 + 24 * c0 + 2 * n_up + m, i, 24), hsrc, LAT, kt=n_up,
                                ready=(hid_ready, At(h_s(l) + 8 * c0, i, 8)) if m == 0 else None)

                with pe.Fori(0, 2) as i:
                    chunk(i, 0, CH)
                chunk(None, 2, NF - 2 * CH)
                ln_stats(2 * l + 1)

        @block.scalar
        def _(act):
            def split_hi(t):
                wait(act, w_raw[t % 4], (t // 4 + 1).times(16))
                wait(act, tile_done, t + -1)
                act.activation(Whi[:, t % 2, :], Wraw[:, t % 4, :], ACT.Copy).then_inc(w_hi, 1)

            def evac(t):
                split_hi(t + 1)
                wait(act, tile_done, t + 1)

            def norm(n, rng, upd, par, which):
                a0, b0 = rng
                for k in range(KD):
                    if n == 0:
                        act.wait_ge(x_in, 32)
                    else:
                        freed(act, At(upd + k))
                    wait(act, sq_used, 8 * n + k - 1)
                    act.activation(SQ[:, k % 2, a0:b0], X[:, k, a0:b0], ACT.Square).then_inc(sq_ready, 1)
                act.wait_ge(sq_used, 8 * n + 8)
                act.activation(RS[:, a0:b0], ps(B4, a0, b0), ACT.Sqrt, scale=1.0 / D,
                               bias=VEC[:, VEC_AT["eps"]:VEC_AT["eps"] + 1]).then_inc(std_ready, 1)
                dst = (h0, h1, h2, h3)[n]
                off = 0 if n < 3 else NC
                for k in range(KD):
                    act.wait_ge(nt_ready, 8 * n + k + 1)
                    for a, b in parts(rng):
                        v = 1 if a == 0 else 0
                        last = act.activation(dst[0][:, k, a - off:b - off], T[:, k % 2, a:b], ACT.Identity,
                                              bias=MOD[:, par, v, which * 24 + k:which * 24 + k + 1])
                    last.then_inc(nhi_ready, 1)

            def mlp(t0, hid, rng, h0_):
                a0, b0 = rng
                off = 0 if rng == FULL else NC

                def chunk(i):
                    for j in range(CH):
                        t = At(t0 + j, i, 16)
                        hn = At(h0_ + j, i, CH)
                        evac(t)
                        act.activation(T[:, j % 2, a0:b0], ps(G[t % 2], a0, b0), ACT.Relu).then_inc(
                            tile_free[t % 2], 1)
                        wait(act, hsq2_ready, hn + 1)
                        act.activation(hid[0][:, j, a0 - off:b0 - off], SQ[:, j % 2, a0:b0],
                                       ACT.Copy).then_inc(hidhi_ready, 1)
                    for m in range(KD):
                        split_hi(At(t0 + CH + m + 1, i, 16))

                with act.Fori(0, HID // P // CH) as i:
                    chunk(i)

            act.wait_ge(c_in, 32)
            act.wait_ge(small_in, 32)
            for v in range(2):
                act.activation(SQ[:, v, 0:NT], CB[:, v, 0:NT], ACT.Sigmoid).then_inc(silu_done, 1)
                act.activation(T[:, v, 0:D - NT], CB[:, v, NT:D], ACT.Sigmoid).then_inc(silu_done, 1)
            act.wait_ge(silu_ready, 4)
            split_hi(At(0))
            act.wait_ge(mods, 1)
            norm(0, FULL, 0, 0, 0)
            a, b = FULL
            for t in range(N_HYB):
                evac(At(t))
                g = ps(G[t % 2], a, b)
                if t == 0:
                    gb = VEC_AT["gate_b"]
                    act.activation(rows[0][0:GW, :], g[0:GW, :], ACT.Identity,
                                   bias=VEC[0:GW, gb:gb + 1]).then_inc(gate_step, 1)
                    act.activation(rows[1][0:GW, :], g[64:64 + GW, :], ACT.Identity,
                                   bias=VEC[64:64 + GW, gb:gb + 1]).then_inc(tile_free[0], 1)
                    act.wait_ge(tile_free[0], 1)
                    act.activation(rows[2][0:GW, :], rows[1][0:GW, :], ACT.Abs).then_inc(gate_step, 1)
                    act.wait_ge(gate_step, 2)
                    act.activation(rows[2][0:GW, :], rows[2][0:GW, :], ACT.Exp, scale=-1.0).then_inc(gate_step, 1)
                    act.wait_ge(gate_step, 3)
                    act.activation(rows[2][0:GW, :], rows[2][0:GW, :], ACT.Ln, bias=1.0).then_inc(gate_step, 1)
                elif t < 3:
                    act.activation(HQ[:, t - 1, :], g, ACT.Copy).then_inc(tile_free[t % 2], 1)
                elif t < 5:
                    act.activation(HK[:, t - 3, :], g, ACT.Copy).then_inc(tile_free[t % 2], 1)
                elif t < 9:
                    n = t - 5
                    wait(act, turned, n - 1)
                    act.activation(T[:, n % 2, 0:NT], g, ACT.Copy).then_inc(tile_free[t % 2], 1)
                elif t < 13:
                    act.activation(SO[:, t - 9, :], g, ACT.Sigmoid).then_inc(tile_free[t % 2], 1)
                elif t < 21 and t % 2 == 1:
                    n = (t - 13) // 2
                    wait(act, cu_done, n - 1)
                    act.activation(SQ[:, n % 2, 0:NT], g, ACT.Copy).then_inc(tile_free[1], 1)
            act.wait_ge(acol_ps, 1)
            act.activation(ACOL[:, :, :], B4[:, 0:TT * GW].rearrange("p (i g) -> p i g", g=GW),
                           ACT.Copy).then_inc(acol_ready, 1)
            act.wait_ge(acol_ready, 1)

            def pieces(d):
                out_ = []
                order = (0, 1, 2, 3, 4, 5) if d == 0 else (1, 0, 5, 4, 3, 2)
                for i in order:
                    if i < 2:
                        out_.append((i, (P * i, NC) if d == 0 else (0, P * (i + 1))))
                        out_.append((i, (NC, NT)))
                    else:
                        out_.append((i, (P * i, NT) if d == 0 else (NC, P * (i + 1))))
                return out_

            for q in range(2 * MH):
                h, d = q // 2, q % 2
                act.wait_ge(m_ps, 2 * q + 1)
                if q > 0:
                    act.wait_ge(d_ready, 8 * q)
                    act.wait_ge(md_ready, q)
                act.activation(Mb[:, :], ps(B4, 0, NT), ACT.Copy).then_inc(m_used, 1)
                act.wait_ge(m_used, 2 * q + 1)
                wait(act, pv_done, q - 1)
                at = 0
                for n, (i, (a, b)) in enumerate(pieces(d)):
                    bias = ACOL[:, i, 32 * d + h:32 * d + h + 1]
                    lo_, hi_ = P * i, P * (i + 1)
                    segs = []
                    if a <= lo_ and hi_ <= b:
                        segs = [(MD, lo_, hi_)]
                        if a < lo_:
                            segs.append((Mb, a, lo_))
                        if hi_ < b:
                            segs.append((Mb, hi_, b))
                    else:
                        segs = [(Mb, a, b)]
                    if n == 0:
                        act.wait_ge(md_ready, q + 1)
                    for src, u, v in segs:
                        last = act.activation(PB[:, d, at + u - a:at + v - a], src[:, u:v], ACT.Exp, bias=bias,
                                              scale=-1.0)
                    last.then_inc(d_ready, 1)
                    at += b - a
                act.wait_ge(m_ps, 2 * q + 2)
                wait(act, nd_used, q)
                act.activation(T[:, 0, 0:NT], ps(B4, 0, NT), ACT.Exp, scale=-1.0).then_inc(m_used, 1)
                if d == 1:
                    act.wait_ge(hsum_ready, h + 1)
                    act.activation(SQ[:, 0, 0:NT], HF[:, :], ACT.Square).then_inc(hsq_ready, 1)
                    act.wait_ge(hstat_done, h + 1)
                    act.activation(RS[:, :], ps(B4, 0, NT), ACT.Sqrt, scale=1.0 / DV,
                                   bias=VEC[:, VEC_AT["eps"]:VEC_AT["eps"] + 1]).then_inc(hstd_ready, 1)
                    act.wait_ge(ht_ready, h + 1)
                    act.activation(mixa[0][:, h, :], HF[:, :], ACT.Copy).then_inc(hhi_ready, 1)
            act.wait_ge(pv_done, 2 * MH)
            for j in range(4):
                act.activation(mixb[0][:, j, 0:NC], CY[:, j, 1:1 + NC], ACT.Copy)
                act.activation(mixb[0][:, j, NC:NT], CY[:, j, 3 + NC:3 + NT], ACT.Copy).then_inc(hhi_ready, 1)
            for m in range(KD):
                split_hi(At(T_HOUT + m + 1))
            norm(1, FULL, T_HOUT, 0, 1)
            mlp(T_MLP0, hid0, FULL, H_M0)
            act.wait_ge(c_in, 48)
            act.wait_ge(hid_ready, 32)
            act.activation(SQ[:, 0, 0:NT], CB[:, 0, 0:NT], ACT.Sigmoid).then_inc(silu_done, 1)
            act.activation(T[:, 0, 0:D - NT], CB[:, 0, NT:D], ACT.Sigmoid).then_inc(silu_done, 1)
            act.wait_ge(silu_ready, 6)
            act.wait_ge(mods, 3)
            norm(2, FULL, T_ATT - KD, 1, 0)
            for t in range(N_ATT):
                evac(At(T_ATT + t))
                g = G[(T_ATT + t) % 2]
                if t < 2:
                    n = 4 + t
                    wait(act, turned, n - 1)
                    act.activation(T[:, n % 2, 0:NT], ps(g, 0, NT), ACT.Copy).then_inc(
                        tile_free[(T_ATT + t) % 2], 1)
                else:
                    n = t - 2
                    a, b = FULL if t < 4 else LAT
                    wait(act, qk_n, n - 1)
                    if n < 2:
                        act.wait_ge(turned, 6)
                    act.activation(T[:, n % 2, a:b], ps(g, a, b), ACT.Copy).then_inc(
                        tile_free[(T_ATT + t) % 2], 1)
                    freed(act, At(T_ATT + t))
                    wait(act, qk_stat, n - 1)
                    act.activation(SQ[:, n % 2, a:b], T[:, n % 2, a:b], ACT.Square).then_inc(qk_sq, 1)
                    if n >= 1:
                        a, b = FULL if n - 1 < 2 else LAT
                        act.wait_ge(qk_stat, n)
                        wait(act, qk_n, n - 1)
                        act.activation(RS[:, a:b], ps(B4, a, b), ACT.Sqrt, scale=1.0 / HD,
                                       bias=VEC[:, VEC_AT["eps"]:VEC_AT["eps"] + 1]).then_inc(qk_std, 1)
            act.wait_ge(qk_stat, 10)
            act.wait_ge(qk_n, 9)
            act.activation(RS[:, NC:NT], ps(B4, NC, NT), ACT.Sqrt, scale=1.0 / HD,
                           bias=VEC[:, VEC_AT["eps"]:VEC_AT["eps"] + 1]).then_inc(qk_std, 1)
            act.wait_ge(qk_ready, 10)
            for it in range(4 * AH + 1):
                if it < 4 * AH:
                    act.wait_ge(amax_ready, it + 1)
                    wait(act, at_done, it - 1)
                    act.activation(PR[:, it % 2, :], G[it % 2][:, 0:NT], ACT.Exp, bias=NM[:, it:it + 1],
                                   accum_out=ZS[:, it:it + 1]).then_inc(aexp_done, 1)
                if it >= 1:
                    n = it - 1
                    hn, qt = n // 4, n % 4
                    act.wait_ge(at_done, n + 1)
                    if qt == 0:
                        wait(act, apv_done, hn - 1)
                    act.activation(PT[:, hn % 2, :, qt * P:(qt + 1) * P],
                                   B4[:, 0:NT].rearrange("p (i t) -> p i t", t=P), ACT.Copy).then_inc(at_used, 1)
                    if n % 8 == 6 and n > 8:
                        j = n // 8 - 1
                        act.wait_ge(apv_done, 2 * j + 2)
                        act.activation(ao[0][:, j, :], B6[:, 512 * (j % 2):512 * (j % 2) + NX],
                                       ACT.Copy).then_inc(ao_hi_ready, 1)
            act.wait_ge(apv_done, AH)
            act.activation(ao[0][:, 7, :], B6[:, 512:1024], ACT.Copy).then_inc(ao_hi_ready, 1)
            for m in range(KD):
                split_hi(At(T_AOUT + m + 1))
            norm(3, LAT, T_AOUT, 1, 1)
            mlp(T_MLP1, hid1, LAT, H_M1)
            def enter_block():
                for k in range(KD):
                    freed(act, At(T_S - KD + k))
                    if k == 0:
                        act.wait_ge(mods, 4)
                    act.activation(hs[0][:, k, :], X[:, k, NC:NT], ACT.Identity, scale=GAIN[:, 0, 0, 0, k:k + 1],
                                   bias=MOD[:, 0, 0, k:k + 1]).then_inc(ln_hi_ready, 1)

            def layer_norm(n):
                for k in range(KD):
                    act.wait_ge(centred, 8 * n + k + 1)
                    wait(act, sq_used, 32 + 8 * n + k - 1)
                    act.activation(SQ[:, k % 2, 0:NX], X[:, k, NC:NT], ACT.Square).then_inc(sq_ready, 1)
                act.wait_ge(sq_used, 32 + 8 * n + 8)
                act.activation(RS[:, 0:NX], B4[:, 512:1024], ACT.Sqrt, scale=1.0 / D,
                               bias=VEC[:, VEC_AT["ln_eps"]:VEC_AT["ln_eps"] + 1]).then_inc(std_ready, 1)
                for k in range(KD):
                    act.wait_ge(ln_t_ready, 8 * n + k + 1)
                    if n < 3:
                        act.activation(hs[0][:, k, :], T[:, k % 2, 0:NX], ACT.Identity,
                                       scale=GAIN[:, n // 2, 1, n % 2, k:k + 1],
                                       bias=OFFS[:, n % 2, k:k + 1]).then_inc(ln_hi_ready, 1)
                    act.activation(X[:, k, NC:NT], T[:, k % 2, 0:NX], ACT.Identity, scale=LNA[:, 0, k:k + 1],
                                   bias=LNA[:, 1, k:k + 1]).then_inc(ln_x_ready, 1)

            enter_block()
            for l in range(2):
                t0 = T_S + l * N_S
                if l == 1:
                    pass
                for t in range(N_MIX):
                    evac(At(t0 + t))
                    g = ps(G[(t0 + t) % 2], NC, NT)
                    free = tile_free[(t0 + t) % 2]
                    if t < 4:
                        n = 4 * l + t
                        wait(act, v_turned, n - 1)
                        act.activation(T[:, n % 2, 0:NX], g, ACT.Gelu_apprx_tanh).then_inc(free, 1)
                    elif t < 8:
                        act.activation(PA[:, t - 4, PAD:PAD + NX], g, ACT.Copy).then_inc(free, 1)
                    else:
                        act.activation(UG[:, t - 8, :], g, ACT.Gelu_apprx_tanh).then_inc(free, 1)
                    if t == 7:
                        act.wait_ge(v_var, l + 1)
                        act.activation(small[:, 24:28], small[:, 16:24].rearrange("p (c s) -> p c s", s=2)[:, :, 1],
                                       ACT.Sqrt, bias=VEC[:, VEC_AT["ln_eps"]:VEC_AT["ln_eps"] + 1]).then_inc(v_std, 1)
                for g in range(SGH):
                    act.wait_ge(pool_done, 4 * l + g + 1)
                    pscale = VEC_AT["pool_scale"] + 4 * l + g
                    act.activation(ms[0][:, g, :], B6[:, 512 * (g % 2):512 * (g % 2) + NX], ACT.Copy,
                                   scale=VEC[:, pscale:pscale + 1]).then_inc(mix_hi, 1)
                for h in range(SGH):
                    act.wait_ge(gated_ready, 4 * l + h + 1)
                    act.activation(ms[0][:, 4 + h, :], T[:, h % 2, 0:NX], ACT.Copy).then_inc(mix_hi, 1)
                for m in range(KD):
                    split_hi(At(t0 + N_MIX + m + 1))
                layer_norm(2 * l)
                t1 = t0 + N_MIX + N_OUT

                def chunk(i, c0, n_up, last=False):
                    for j in range(n_up):
                        t = At(t1 + 24 * c0 + 2 * j, i, 24)
                        fn = At(NF * l + 8 * c0 + j, i, 8)
                        evac(t)
                        act.activation(GP[:, j % 2, 2:2 + NX], ps(G[t % 2], NC, NT), ACT.Copy).then_inc(
                            tile_free[t % 2], 1)
                        split_hi(t + 2)
                        wait(act, ffconv, fn.times(2) + 2)
                        act.activation(T[:, j % 2, 0:NX], CV[:, j % 2, :], ACT.Gelu_apprx_tanh).then_inc(ffgelu, 1)
                        freed(act, t + 1)
                        act.activation(hid2[0][:, j, :], SQ[:, j % 2, 0:NX], ACT.Copy).then_inc(ffhi, 1)
                    for m in range(KD):
                        t = At(t1 + 24 * c0 + 2 * n_up + m + 1, i, 24)
                        if not (last and m == KD - 1 and l == 1):
                            split_hi(t)

                with act.Fori(0, 2) as i:
                    chunk(i, 0, CH)
                chunk(None, 2, NF - 2 * CH, last=True)
                layer_norm(2 * l + 1)

        @block.vector
        def _(dve):
            links = [0]

            def link(ins):
                links[0] += 1
                ins.then_inc(vlink, 1)
                dve.wait_ge(vlink, links[0])

            def split_lo(t):
                wait(dve, w_hi, t + 1)
                dve.tensor_tensor(Wlo[:, t % 2, :], Wraw[:, t % 4, :], Whi[:, t % 2, :].bitcast(F32),
                                  ALU.subtract).then_inc(w_lo, 1)

            def evac(t):
                split_lo(t + 1)
                wait(dve, tile_done, t + 1)

            def ada(n, col, par, vectors):
                wait(dve, ada_raw[n % 2], (n // 2 + 1).times(16))
                for v in range(vectors):
                    o = MRAW[:, par, v, col.c:col.c + 1] if col.i is None else MRAW[:, par, v, bass.ds(col.value(), 1)]
                    if v + 1 < vectors:
                        wait(dve, ada_used, n)
                    last = dve.scalar_tensor_tensor(out=Araw[:, n % 2, :] if v + 1 == vectors else Junk[:, :], in0=Araw[:, n % 2, :], scalar=1.0, in1=CB[:, v, :],
                                                    op0=ALU.mult, op1=ALU.mult, accum_out=o)
                last.then_inc(ada_used, 1)

            def vec(name, n=0, w=1):
                return VEC[:, VEC_AT[name] + n:VEC_AT[name] + n + w]

            def add_bias(layer, par, vectors, a, b):
                for v in range(vectors):
                    link(dve.tensor_tensor(MOD[:, par, v, a:b], MRAW[:, par, v, a:b], vec("ada_b", ADA * layer + a, b - a),
                                           ALU.add))

            def gains(layer, par, which, vectors):
                for v in range(vectors):
                    link(dve.scalar_tensor_tensor(out=GAIN[:, par, which, v, :],
                                                  in0=MOD[:, par, v, 24 * which + 8:24 * which + 16], scalar=1.0,
                                                  in1=vec(("norm1_g", "norm2_g")[which], 8 * layer, 8),
                                                  op0=ALU.add, op1=ALU.mult))

            def norm(n, rng, par, which):
                a0, b0 = rng
                off = 0 if n < 3 else NC
                dst = (h0, h1, h2, h3)[n]
                dve.wait_ge(std_ready, n + 1)
                dve.reciprocal(RS[:, a0:b0], RS[:, a0:b0]).then_inc(rstd_ready, 1)
                dve.wait_ge(rstd_ready, n + 1)

                def scaled(k):
                    wait(dve, nhi_ready, 8 * n + k - 1)
                    wait(dve, src_ready, 8 * (S_N0, S_N1, S_N2, S_N3)[n] + k - 1)
                    for a, b in parts(rng):
                        v = 1 if a == 0 else 0
                        last = dve.scalar_tensor_tensor(out=T[:, k % 2, a:b], in0=X[:, k, a:b],
                                                        scalar=GAIN[:, par, which, v, k:k + 1], in1=RS[:, a:b],
                                                        op0=ALU.mult, op1=ALU.mult)
                    last.then_inc(nt_ready, 1)

                scaled(0)
                for k in range(KD):
                    if k + 1 < KD:
                        scaled(k + 1)
                    dve.wait_ge(nhi_ready, 8 * n + k + 1)
                    for a, b in parts(rng):
                        v = 1 if a == 0 else 0
                        last = dve.scalar_tensor_tensor(out=dst[1][:, k, a - off:b - off], in0=T[:, k % 2, a:b],
                                                        scalar=MOD[:, par, v, which * 24 + k:which * 24 + k + 1],
                                                        in1=dst[0][:, k, a - off:b - off].bitcast(F32),
                                                        op0=ALU.add, op1=ALU.subtract)
                    last.then_inc(src_ready, 1)

            def add_residual(t, m, rng, par, gate):
                evac(t)
                for a, b in parts(rng):
                    v = 1 if a == 0 else 0
                    last = dve.scalar_tensor_tensor(out=X[:, m, a:b], in0=ps(G[t % 2], a, b),
                                                    scalar=MOD[:, par, v, gate * 8 + m:gate * 8 + m + 1],
                                                    in1=X[:, m, a:b], op0=ALU.mult, op1=ALU.add)
                last.then_inc(tile_free[t % 2], 1)

            def mlp(t0, hid, rng, h0_, par, ada_layer, ada_par, vectors):
                a0, b0 = rng
                off = 0 if rng == FULL else NC
                with dve.Fori(0, HID // P // CH) as i:
                    done = 0

                    def step(j):
                        nonlocal done
                        if j % 4:
                            ada(At(ADA * ada_layer + done, i, 12), At(done, i, 12), ada_par, vectors)
                            done += 1

                    for j in range(CH):
                        t = At(t0 + j, i, 16)
                        hn = At(h0_ + j, i, CH)
                        split_lo(t + 1)
                        step(j)
                        freed(dve, t)
                        dve.tensor_tensor(SQ[:, j % 2, a0:b0], T[:, j % 2, a0:b0], T[:, j % 2, a0:b0],
                                          ALU.mult).then_inc(hsq2_ready, 1)
                        wait(dve, hidhi_ready, hn + 1)
                        dve.tensor_tensor(hid[1][:, j, a0 - off:b0 - off], SQ[:, j % 2, a0:b0],
                                          hid[0][:, j, a0 - off:b0 - off].bitcast(F32),
                                          ALU.subtract).then_inc(hid_ready, 1)
                    for m in range(KD):
                        add_residual(At(t0 + CH + m, i, 16), m, rng, par, 5)
                        step(CH + m)

            for v in range(2):
                dve.wait_ge(silu_done, 2 * v + 2)
                dve.tensor_tensor(CB[:, v, 0:NT], CB[:, v, 0:NT], SQ[:, v, 0:NT], ALU.mult).then_inc(silu_ready, 1)
                dve.tensor_tensor(CB[:, v, NT:D], CB[:, v, NT:D], T[:, v, 0:D - NT], ALU.mult).then_inc(silu_ready, 1)
            dve.wait_ge(silu_ready, 4)
            split_lo(At(0))
            for n in range(16):
                ada(At(n), At(n), 0, 2)
            dve.wait_ge(ada_used, 16)
            add_bias(0, 0, 2, 0, 16)
            gains(0, 0, 0, 2)
            dve.sem_inc(mods, 1)
            norm(0, FULL, 0, 0)
            R = [r[0:GW, :] for r in rows]

            def step(ins, n):
                ins.then_inc(gate_step, 1)
                dve.wait_ge(gate_step, n)

            def flip(dst, src, n):
                dve.tensor_copy(dst[0:32, :], src[0:32, :])
                dve.tensor_copy(dst[32:GW, 0:NC], src[32:GW, 0:NC][:, ::-1])
                step(dve.tensor_copy(dst[32:GW, NC:NT], src[32:GW, NC:NT][:, ::-1]), n)

            def gate_chain(part):
                if part == 0:
                    dve.wait_ge(gate_step, 4)
                    step(dve.scalar_tensor_tensor(out=R[1], in0=R[1], scalar=0.0, in1=R[2], op0=ALU.min,
                                                  op1=ALU.subtract), 5)
                    flip(R[2], R[1], 6)
                    step(dve.tensor_tensor_scan(R[1], ones[0:GW, 0:1].to_broadcast([GW, NT]), R[2], 0.0, ALU.mult,
                                                ALU.add), 7)
                    flip(R[2], R[0], 8)
                    step(dve.tensor_tensor(R[2], R[2], R[1], ALU.subtract), 9)
                    step(dve.tensor_tensor_scan(R[0], R[2], R[2], 0.0, ALU.max, ALU.max), 10)
                if part == 1:
                    step(dve.tensor_tensor(R[1], R[1], R[0], ALU.add), 11)
                    flip(RM[0:GW, :], R[0], 12)
                    flip(R[0], R[1], 13)
                    step(dve.tensor_copy(RM[64:64 + GW, :], R[0]), 14)
                    flip(R[1], R[2], 15)

            for t in range(N_HYB):
                if 13 <= t < 21 and t % 2 == 0 or t >= 21:
                    evac(At(t))
                else:
                    split_lo(At(t + 1))
                g = G[t % 2]
                if t in (1, 3):
                    gate_chain(t // 2)
                if 6 <= t < 10:
                    n = t - 6
                    dve.wait_ge(turned, n + 1)
                    dve.tensor_copy(HV[:, :, n * P:(n + 1) * P],
                                    B6[:, 0:NT].rearrange("p (i c) -> p i c", c=P)).then_inc(turn_used, 1)
                if 13 <= t < 21 and t % 2 == 0:
                    j = (t - 13) // 2
                    freed(dve, At(t - 1))
                    if j == 0:
                        dve.wait_ge(turned, 4)
                        link(dve.memset(T[:, 0, :], 0.0))
                    dve.tensor_tensor(T[:, 0, 1:1 + NC], SQ[:, j % 2, 0:NC], ps(g, 0, NC), ALU.mult)
                    link(dve.tensor_tensor(T[:, 0, 3 + NC:3 + NT], SQ[:, j % 2, NC:NT], ps(g, NC, NT), ALU.mult))
                    dve.sem_inc(tile_free[t % 2], 1)
                    dve.sem_inc(cu_done, 1)
                    y = CY[:, j, 1:771]
                    link(dve.tensor_scalar(y, T[:, 0, 0:770], vec("conv_w", j), None, ALU.mult))
                    for k in (1, 2):
                        link(dve.scalar_tensor_tensor(out=y, in0=T[:, 0, k:k + 770], scalar=vec("conv_w", 4 * k + j),
                                                      in1=y, op0=ALU.mult, op1=ALU.add))
                if t >= 21:
                    j = t - 21
                    dve.tensor_tensor(CY[:, j, 1:1 + NC], CY[:, j, 1:1 + NC], ps(g, 0, NC), ALU.mult)
                    link(dve.tensor_tensor(CY[:, j, 3 + NC:3 + NT], CY[:, j, 3 + NC:3 + NT], ps(g, NC, NT), ALU.mult))
                    dve.sem_inc(tile_free[t % 2], 1)
                if t < 16:
                    for n in (16 + 2 * t, 17 + 2 * t):
                        ada(At(n), At(n), 0, 2)
            dve.wait_ge(ada_used, ADA)
            add_bias(0, 0, 2, 16, ADA)
            gains(0, 0, 1, 2)
            dve.sem_inc(mods, 1)
            def pieces(d):
                out_ = []
                order = (0, 1, 2, 3, 4, 5) if d == 0 else (1, 0, 5, 4, 3, 2)
                for i in order:
                    if i < 2:
                        out_.append((i, (P * i, NC) if d == 0 else (0, P * (i + 1))))
                        out_.append((i, (NC, NT)))
                    else:
                        out_.append((i, (P * i, NT) if d == 0 else (NC, P * (i + 1))))
                return out_

            for q in range(2 * MH):
                h, d = q // 2, q % 2
                dve.wait_ge(m_used, 2 * q + 1)
                wait(dve, d_ready, 8 * q)
                mask = (mask_f, mask_b)[d]
                dve.tensor_tensor(MD[:, :].rearrange("p (i t) -> p i t", t=P), Mb[:, :].rearrange("p (i t) -> p i t", t=P),
                                  mask.unsqueeze(1).broadcast_to([P, TT, P]), ALU.add).then_inc(md_ready, 1)
                at = 0
                for n, (i, (a, b)) in enumerate(pieces(d)):
                    r = 8 * q + n
                    dve.wait_ge(sc_done, r + 1)
                    dve.wait_ge(d_ready, r + 1)
                    dve.scalar_tensor_tensor(out=PB[:, d, at:at + b - a],
                                             in0=G[0][:, 512 * (r % 2):512 * (r % 2) + b - a], scalar=DK ** -0.5,
                                             in1=PB[:, d, at:at + b - a], op0=ALU.mult, op1=ALU.mult).then_inc(p_ready, 1)
                    at += b - a
                dve.wait_ge(pv_done, q + 1)
                dve.wait_ge(m_used, 2 * q + 2)
                link(dve.tensor_tensor(T[:, 1, 0:NT], ps(G[1], 0, NT), T[:, 0, 0:NT], ALU.max))
                link(dve.scalar_tensor_tensor(out=T[:, 1, 0:NT], in0=ps(G[1], 0, NT), scalar=-1.0, in1=T[:, 1, 0:NT],
                                              op0=ALU.mult, op1=ALU.max))
                link(dve.reciprocal(T[:, 1, 0:NT], T[:, 1, 0:NT]))
                if d == 0:
                    link(dve.tensor_tensor(HF[:, :], ps(B6, 0, NT), T[:, 1, 0:NT], ALU.mult))
                    dve.sem_inc(nd_used, 1)
                else:
                    link(dve.tensor_tensor(T[:, 1, 0:NT], ps(B6, 0, NT), T[:, 1, 0:NT], ALU.mult))
                    dve.sem_inc(nd_used, 1)
                    link(dve.tensor_tensor(HF[:, :], HF[:, :], T[:, 1, 0:NT], ALU.add))
                    dve.sem_inc(hsum_ready, 1)
                    dve.wait_ge(hstd_ready, h + 1)
                    link(dve.reciprocal(RS[:, :], RS[:, :]))
                    link(dve.scalar_tensor_tensor(out=HF[:, :], in0=HF[:, :], scalar=vec("mnorm_g", h), in1=RS[:, :],
                                                  op0=ALU.mult, op1=ALU.mult))
                    link(dve.tensor_tensor(HF[:, :], HF[:, :], SO[:, h, :], ALU.mult))
                    dve.sem_inc(ht_ready, 1)
                    dve.wait_ge(hhi_ready, h + 1)
                    dve.tensor_tensor(mixa[1][:, h, :], HF[:, :], mixa[0][:, h, :].bitcast(F32),
                                      ALU.subtract).then_inc(src_ready, 1)
            for j in range(4):
                dve.wait_ge(hhi_ready, MH + j + 1)
                dve.tensor_tensor(mixb[1][:, j, 0:NC], CY[:, j, 1:1 + NC], mixb[0][:, j, 0:NC].bitcast(F32), ALU.subtract)
                dve.tensor_tensor(mixb[1][:, j, NC:NT], CY[:, j, 3 + NC:3 + NT], mixb[0][:, j, NC:NT].bitcast(F32),
                                  ALU.subtract).then_inc(src_ready, 1)
            for m in range(KD):
                add_residual(At(T_HOUT + m), m, FULL, 0, 2)
            norm(1, FULL, 0, 1)
            mlp(T_MLP0, hid0, FULL, H_M0, 0, 1, 1, 2)
            dve.wait_ge(ada_used, 2 * ADA)
            dve.sem_inc(cb_free, 1)
            add_bias(1, 1, 2, 0, ADA)
            gains(1, 1, 0, 2)
            gains(1, 1, 1, 2)
            dve.sem_inc(mods, 1)
            dve.wait_ge(silu_done, 6)
            dve.tensor_tensor(CB[:, 0, 0:NT], CB[:, 0, 0:NT], SQ[:, 0, 0:NT], ALU.mult).then_inc(silu_ready, 1)
            dve.tensor_tensor(CB[:, 0, NT:D], CB[:, 0, NT:D], T[:, 0, 0:D - NT], ALU.mult).then_inc(silu_ready, 1)
            dve.wait_ge(silu_ready, 6)
            norm(2, FULL, 1, 0)

            def qk_finish(n):
                rng = FULL if n < 2 else LAT
                a, b = rng
                dve.wait_ge(qk_std, n + 1)
                link(dve.reciprocal(RS[:, a:b], RS[:, a:b]))
                if n < 2:
                    gain = vec("k_g")
                else:
                    gain = small[:, 0:1]
                wait(dve, rot_done, n - 1)
                dve.scalar_tensor_tensor(out=QN[:, n % 2, a:b], in0=T[:, n % 2, a:b], scalar=gain, in1=RS[:, a:b],
                                         op0=ALU.mult, op1=ALU.mult).then_inc(qk_n, 1)
                dve.wait_ge(qk_n, n + 1)
                if n < 2:
                    dve.tensor_copy(AK[:, n, 0:NC], QN[:, n % 2, 0:NC])

            def qk_turn(n):
                dst = AK[:, n, NC:NT] if n < 2 else AQ[:, n - 2, :]
                link(dve.tensor_tensor(RT[:, :], QN[:, n % 2, NC:NT], ROPE[:, 0, :], ALU.mult))
                dve.wait_ge(rot_done, n + 1)
                link(dve.tensor_tensor(dst, B6[:, 0:NX], ROPE[:, 1, :], ALU.mult))
                dve.tensor_tensor(dst, dst, RT[:, :], ALU.add).then_inc(qk_ready, 1)

            link(dve.tensor_scalar(small[:, 0:1], vec("q_g"), HD ** -0.5, None, ALU.mult))
            for t in range(N_ATT):
                split_lo(At(T_ATT + t + 1))
                if 1 <= t < 3:
                    n = 4 + t - 1
                    dve.wait_ge(turned, n + 1)
                    dve.tensor_copy(AV[:, :, (n - 4) * P:(n - 3) * P],
                                    B6[:, 0:NT].rearrange("p (i c) -> p i c", c=P)).then_inc(turn_used, 1)
                if t == 4:
                    dve.wait_ge(late_in, 16)
                if t >= 3:
                    if t >= 4:
                        qk_turn(t - 4)
                    qk_finish(t - 3)
            qk_turn(8)
            qk_finish(9)
            qk_turn(9)
            for it in range(4 * AH):
                dve.wait_ge(as_done, it + 1)
                dve.tensor_reduce(NM[:, it:it + 1], G[it % 2][:, 0:NT], AX.X, ALU.max, negate=True).then_inc(amax_ready, 1)
                dve.wait_ge(aexp_done, it + 1)
                link(dve.reciprocal(ZR[:, it:it + 1], ZS[:, it:it + 1]))
                dve.tensor_scalar(PR[:, it % 2, :], PR[:, it % 2, :], ZR[:, it:it + 1], None,
                                  ALU.mult).then_inc(aprob_ready, 1)
                if it % 8 == 7 and it > 8:
                    j = it // 8 - 1
                    dve.wait_ge(ao_hi_ready, j + 1)
                    dve.tensor_tensor(ao[1][:, j, :], B6[:, 512 * (j % 2):512 * (j % 2) + NX],
                                      ao[0][:, j, :].bitcast(F32), ALU.subtract).then_inc(src_ready, 1)
            dve.wait_ge(ao_hi_ready, 8)
            dve.tensor_tensor(ao[1][:, 7, :], B6[:, 512:1024], ao[0][:, 7, :].bitcast(F32),
                              ALU.subtract).then_inc(src_ready, 1)
            for m in range(KD):
                add_residual(At(T_AOUT + m), m, LAT, 1, 2)
            norm(3, LAT, 1, 1)
            mlp(T_MLP1, hid1, LAT, H_M1, 1, 2, 0, 1)
            def fold(l):
                add_bias(2 + l, l, 1, 0, ADA)
                link(dve.tensor_scalar(GAIN[:, l, 0, 0, :], MOD[:, l, 0, 8:16], 1.0, None, ALU.add))
                link(dve.tensor_scalar(GAIN[:, l, 0, 1, :], MOD[:, l, 0, 32:40], 1.0, None, ALU.add))

            def fold_norm(n, lng, lnb, ln, nxt, which):
                if nxt is not None:
                    scale1, shift = GAIN[:, nxt, 0, which, :], MOD[:, nxt, 0, 24 * which:24 * which + 8]
                    link(dve.tensor_tensor(GAIN[:, n // 2, 1, n % 2, :], scale1, vec(lng, 8 * ln, 8), ALU.mult))
                    link(dve.tensor_tensor(OFFS[:, n % 2, :], scale1, vec(lnb, 8 * ln, 8), ALU.mult))
                    link(dve.tensor_tensor(OFFS[:, n % 2, :], OFFS[:, n % 2, :], shift, ALU.add))
                f = ALPHA if nxt is not None else 1.0
                link(dve.tensor_scalar(LNA[:, 0, :], vec(lng, 8 * ln, 8), f, None, ALU.mult))
                link(dve.tensor_scalar(LNA[:, 1, :], vec(lnb, 8 * ln, 8), f, None, ALU.mult))

            dve.wait_ge(ada_used, 3 * ADA)
            fold(0)
            dve.sem_inc(mods, 1)
            for k in range(KD):
                freed(dve, At(T_S - KD + k))
                dve.wait_ge(ln_hi_ready, k + 1)
                link(dve.tensor_scalar(T[:, 0, 0:NX], X[:, k, NC:NT], GAIN[:, 0, 0, 0, k:k + 1], MOD[:, 0, 0, k:k + 1],
                                       ALU.mult, ALU.add))
                link(dve.tensor_tensor(hs[1][:, k, :], T[:, 0, 0:NX], hs[0][:, k, :].bitcast(F32), ALU.subtract))
                dve.sem_inc(src_ready, 1)
                dve.tensor_scalar(X[:, k, NC:NT], X[:, k, NC:NT], ALPHA, None, ALU.mult)

            def layer_norm(n):
                l = n // 2
                dve.wait_ge(mean_done, n + 1)
                link(dve.tensor_scalar(RS[:, 0:NX], B4[:, 512:1024], 1.0 / D, None, ALU.mult))
                for k in range(KD):
                    dve.tensor_tensor(X[:, k, NC:NT], X[:, k, NC:NT], RS[:, 0:NX], ALU.subtract).then_inc(centred, 1)
                dve.wait_ge(centred, 8 * n + 8)
                dve.wait_ge(std_ready, 4 + n + 1)
                link(dve.reciprocal(RS[:, 0:NX], RS[:, 0:NX]))
                for k in range(KD):
                    if n < 3:
                        wait(dve, src_ready, 8 * (s_set(l, 2) if n % 2 == 0 else s_set(1, 0)) + k - 1)
                    dve.wait_ge(ln_x_ready, 8 * n + k - 1) if 8 * n + k - 1 > 0 else None
                    dve.tensor_tensor(T[:, k % 2, 0:NX], X[:, k, NC:NT], RS[:, 0:NX], ALU.mult).then_inc(ln_t_ready, 1)
                    if n < 3:
                        dve.wait_ge(ln_t_ready, 8 * n + k + 1)
                        link(dve.tensor_scalar(SQ[:, k % 2, 0:NX], T[:, k % 2, 0:NX], GAIN[:, l, 1, n % 2, k:k + 1],
                                               OFFS[:, n % 2, k:k + 1], ALU.mult, ALU.add))
                        dve.wait_ge(ln_hi_ready, 8 + 8 * n + k + 1)
                        dve.tensor_tensor(hs[1][:, k, :], SQ[:, k % 2, 0:NX], hs[0][:, k, :].bitcast(F32),
                                          ALU.subtract).then_inc(src_ready, 1)

            for l in range(2):
                t0 = T_S + l * N_S
                for t in range(N_MIX):
                    split_lo(At(t0 + t + 1))
                    if t == 0:
                        dve.wait_ge(src_ready, 8 * s_set(l, 0) + 8)
                        dve.memset(PA[:, :, 0:PAD], 0.0)
                        dve.memset(PS[:, :, 0:PAD], 0.0)
                        dve.wait_ge(late_in, 16 + 48 * (l + 1))
                        for h in range(SGH):
                            last = dve.tensor_tensor(SW[:, h, :], SW[:, h, :], tri, ALU.mult)
                        last.then_inc(tri_ready, 1)
                    if 1 <= t < 5:
                        n = 4 * l + t - 1
                        dve.wait_ge(v_turned, n + 1)
                        dve.tensor_copy(VT[:, :, (t - 1) * P:t * P],
                                        B6[:, 0:NX].rearrange("p (i c) -> p i c", c=P)).then_inc(v_turn_used, 1)
                    if t == 5:
                        dve.wait_ge(v_turn_used, 4 * l + 4)
                        for c in range(4):
                            link(dve.bn_stats(SQ[:, 0, 8 * c:8 * c + 6], VT[:, c, :]))
                            last = dve.bn_aggr(small[:, 16 + 2 * c:18 + 2 * c], SQ[:, 0, 8 * c:8 * c + 6])
                        last.then_inc(v_var, 1)
                    if t == 8:
                        dve.wait_ge(v_std, l + 1)
                        link(dve.reciprocal(small[:, 28:32], small[:, 24:28]))
                        for c in range(4):
                            link(dve.tensor_scalar(VT[:, c, :], VT[:, c, :], small[:, 16 + 2 * c:17 + 2 * c],
                                                   small[:, 28 + c:29 + c], ALU.subtract, ALU.mult))
                            link(dve.tensor_tensor(VT[:, c, :], VT[:, c, :], ROW[:, 0, :], ALU.mult))
                            link(dve.tensor_tensor(VT[:, c, :], VT[:, c, :], ROW[:, 1, :], ALU.add))
                        dve.sem_inc(v_normed, 1)
                for g, w in enumerate(POOL_W):
                    freed(dve, At(t0 + 4 + g))
                    src_ = PA[:, g, :]
                    for e in range(g + 1):
                        link(dve.tensor_tensor(PS[:, e % 2, PAD:], src_[:, PAD:], src_[:, PAD - 2 ** e:PAD + NX - 2 ** e],
                                               ALU.add))
                        src_ = PS[:, e % 2, :]
                    if g:
                        dve.wait_ge(pool_done, 4 * l + g)
                    link(dve.scalar_tensor_tensor(out=PO[:, :], in0=src_[:, PAD:], scalar=1.0 / w, in1=PA[:, g, PAD:],
                                                  op0=ALU.mult, op1=ALU.subtract))
                    link(dve.tensor_tensor(small[:, 0:16], src_[:, PAD:PAD + 16], CON[:, C_RC + 16 * g:C_RC + 16 * (g + 1)],
                                           ALU.mult))
                    dve.tensor_tensor(PO[:, 0:16], small[:, 0:16], PA[:, g, PAD:PAD + 16], ALU.subtract).then_inc(pooled, 1)
                    dve.wait_ge(mix_hi, 8 * l + g + 1)
                    dve.scalar_tensor_tensor(out=ms[1][:, g, :], in0=B6[:, 512 * (g % 2):512 * (g % 2) + NX],
                                             scalar=vec("pool_scale", 4 * l + g), in1=ms[0][:, g, :].bitcast(F32),
                                             op0=ALU.mult, op1=ALU.subtract).then_inc(src_ready, 1)
                for h in range(SGH):
                    dve.wait_ge(gated_ps, 4 * l + h + 1)
                    freed(dve, At(t0 + 8 + h))
                    bias = ROW[:, 2, h * P:(h + 1) * P].unsqueeze(1).broadcast_to([P, 4, P])
                    link(dve.tensor_tensor(T[:, h % 2, 0:NX].rearrange("p (c t) -> p c t", t=P),
                                           B6[:, 512 * (h % 2):512 * (h % 2) + NX].rearrange("p (c t) -> p c t", t=P),
                                           bias, ALU.add))
                    dve.tensor_tensor(T[:, h % 2, 0:NX], T[:, h % 2, 0:NX], UG[:, h, :], ALU.mult).then_inc(gated_ready, 1)
                    dve.wait_ge(mix_hi, 8 * l + 4 + h + 1)
                    dve.tensor_tensor(ms[1][:, 4 + h, :], T[:, h % 2, 0:NX], ms[0][:, 4 + h, :].bitcast(F32),
                                      ALU.subtract).then_inc(src_ready, 1)
                for m in range(KD):
                    add_residual(At(t0 + N_MIX + m), m, LAT, l, 2)
                fold_norm(2 * l, "ln1_g", "ln1_b", l, l, 1)
                layer_norm(2 * l)
                t1 = t0 + N_MIX + N_OUT
                dve.wait_ge(tile_done, t1)
                link(dve.memset(GP[:, :, 0:2], 0.0))

                def chunk(i, c0, n_up, last=False):
                    done_ = 24 * c0

                    def more(n, count):
                        if l == 0:
                            for e in range(count):
                                ada(At(3 * ADA + n + e, i, 16), At(n + e, i, 16), 1, 1)

                    for j in range(n_up):
                        t = At(t1 + 24 * c0 + 2 * j, i, 24)
                        fn = At(NF * l + 8 * c0 + j, i, 8)
                        split_lo(t + 1)
                        if j < 8 and c0 == 0:
                            more(j, 1)
                        elif c0:
                            more(32 + j, 1)
                        freed(dve, t)
                        cw = VEC_AT["ff_conv_w"] + 3 * NF * l
                        cb = VEC_AT["ff_conv_b"] + NF * l

                        def col(base):
                            n = base + 8 * c0 + j
                            return VEC[:, n:n + 1] if i is None else VEC[:, bass.ds(i * 8 + n, 1)]

                        y = CV[:, j % 2, :]
                        dve.tensor_scalar(y, GP[:, j % 2, 2:2 + NX], col(cw + 2 * NF), col(cb), ALU.mult,
                                          ALU.add).then_inc(ffconv0, 1)
                        wait(dve, ffconv0, fn + 1)
                        dve.scalar_tensor_tensor(out=y, in0=GP[:, j % 2, 1:1 + NX], scalar=col(cw + NF), in1=y,
                                                 op0=ALU.mult, op1=ALU.add).then_inc(ffconv, 1)
                        wait(dve, ffconv, fn.times(2) + 1)
                        dve.scalar_tensor_tensor(out=y, in0=GP[:, j % 2, 0:NX], scalar=col(cw), in1=y,
                                                 op0=ALU.mult, op1=ALU.add).then_inc(ffconv, 1)
                        split_lo(t + 2)
                        wait(dve, tile_done, t + 2)
                        wait(dve, ffgelu, fn + 1)
                        dve.tensor_tensor(SQ[:, j % 2, 0:NX], T[:, j % 2, 0:NX], ps(G[(t + 1) % 2], NC, NT),
                                          ALU.mult).then_inc(tile_free[(t + 1) % 2], 1)
                        wait(dve, ffhi, fn + 1)
                        dve.tensor_tensor(hid2[1][:, j, :], SQ[:, j % 2, 0:NX], hid2[0][:, j, :].bitcast(F32),
                                          ALU.subtract).then_inc(hid_ready, 1)
                    for m in range(KD):
                        t = At(t1 + 24 * c0 + 2 * n_up + m, i, 24)
                        if not (last and l == 1 and m == KD - 1):
                            split_lo(t + 1)
                        wait(dve, tile_done, t + 1)
                        dve.scalar_tensor_tensor(out=X[:, m, NC:NT], in0=ps(G[t % 2], NC, NT),
                                                 scalar=MOD[:, l, 0, 40 + m:41 + m], in1=X[:, m, NC:NT],
                                                 op0=ALU.mult, op1=ALU.add).then_inc(tile_free[t % 2], 1)
                        if c0 == 0:
                            more(8 + m, 1)
                        else:
                            more(38 + m + (m == 7), 1 if m < 6 else 2)

                with dve.Fori(0, 2) as i:
                    chunk(i, 0, CH)
                chunk(None, 2, NF - 2 * CH, last=True)
                if l == 0:
                    dve.wait_ge(ada_used, 4 * ADA)
                    fold(1)
                    fold_norm(1, "ln2_g", "ln2_b", 0, 1, 0)
                else:
                    fold_norm(3, "ln2_g", "ln2_b", 1, None, 0)
                layer_norm(2 * l + 1)


def pack(x):
    f = lambda a: np.ascontiguousarray(np.asarray(a), dtype=np.float32)
    cols = lambda a: f(a).reshape(-1, P).T
    xin = np.concatenate([f(x["ctx"])[0], f(x["x"])[0]], 0)
    xin = f(xin.T.reshape(KD, P, NT).transpose(1, 0, 2))

    def units(w, kt=KD):
        w = f(w)
        if w.shape[0] < KD * P:
            w = np.concatenate([w, np.zeros((KD * P - w.shape[0], w.shape[1]), np.float32)], 0)
        return w.reshape(KD, P, -1, P).transpose(2, 1, 0, 3).reshape(-1, P, KD * P)

    def mlp(w1, w2):
        out = []
        for c in range(HID // D):
            out += [units(w1[:, c * D:(c + 1) * D]), units(w2[c * D:(c + 1) * D])]
        return out

    w = f(x["hyb_w_in"])[0]
    at = np.cumsum([0, 256, 256, 512, 512, 16, 512, 512, 512])
    q, k, v, o, g, gb, gc, u = [w[:, a:b] for a, b in zip(at[:-1], at[1:])]
    gates = np.zeros((D, P), np.float32)
    for n, c in enumerate((0, 64, 32, 96)):
        gates[:, c:c + 4] = g[:, 4 * n:4 * n + 4]
    ws = [units(gates), units(q), units(k), units(v), units(o),
          np.stack([units(gc), units(u)], 1).reshape(-1, P, D), units(gb), units(f(x["hyb_w_out"])[0])]
    ws += mlp(f(x["mlp_w1"])[0], f(x["mlp_w2"])[0])
    w = f(x["att_w_in"])[0]
    heads = [h for j in range(8) for h in (8 * (j // 4) + j % 4, 8 * (j // 4) + j % 4 + 4)]
    order = np.concatenate([np.arange(HD * h, HD * (h + 1)) for h in heads])
    ws += [units(w[:, 1280:1536]), units(w[:, 1024:1280]), units(w[:, order]), units(f(x["att_w_out"])[0][order])]
    ws += mlp(f(x["mlp_w1"])[1], f(x["mlp_w2"])[1])
    for l in range(2):
        w = f(x["w_in_2"])[l]
        ws += [units(w[:, 1024:1536]), units(w[:, 0:512]), units(w[:, 512:1024]), units(f(x["w_out_2"])[l])]
        up, down = f(x["w_up_2"])[l], f(x["w_down_2"])[l]
        pairs = np.stack([units(up[:, 0:FF]), units(up[:, FF:])], 1)
        for a, b in ((0, 8), (8, 16), (16, NF)):
            ws += [pairs[a:b].reshape(-1, P, D), units(down[a * P:b * P])]
    wstream = np.concatenate(ws, 0)
    assert wstream.shape[0] == N_UNITS
    adaw = np.concatenate([f(x["ada_w"]), f(x["ada_w_2"])], 0).transpose(0, 2, 1).reshape(4 * ADA, P, D)
    rep = lambda a: np.broadcast_to(f(a), (P,) + np.shape(a))
    cvec = f(np.stack([rep(x["c"][0]), rep(x["c_ctx"]), rep(x["c_2"][0])], 0))
    gate_b = np.zeros((P, 1), np.float32)
    for n, c in enumerate((0, 64, 32, 96)):
        gate_b[c:c + 4, 0] = f(x["hyb_gate_b"])[0, 4 * n:4 * n + 4]
    vecs = np.concatenate([
        cols(x["ada_b"]), cols(x["ada_b_2"]), cols(x["norm1_g"]), cols(x["norm2_g"]), gate_b,
        cols(x["mlstm_norm_g"]), cols(x["conv_w"]), cols(np.concatenate([f(x["q_norm_g"])[0]] * 2)),
        cols(np.concatenate([f(x["k_norm_g"])[0]] * 2)), cols(x["pool_scale_2"]), cols(x["ln1_g_2"]),
        cols(x["ln1_b_2"]), cols(x["ln2_g_2"]), cols(x["ln2_b_2"]), cols(x["conv_w_2"]), cols(x["conv_b_2"]),
        np.full((P, 1), EPS, np.float32), np.full((P, 1), LN_EPS, np.float32)], 1)
    assert vecs.shape[1] == VEC_N
    poolw = f(x["pool_w_2"]).transpose(0, 2, 1, 3)
    sguw = f(x["sgu_w_2"]).transpose(0, 3, 1, 2)
    rows = np.stack([f(x["sgu_ln_g_2"]), f(x["sgu_ln_b_2"]), f(x["sgu_b_2"]).reshape(2, -1)], 1)
    rows = np.broadcast_to(rows[:, None], (2, P, 3, NX))
    return dict(xin=xin, cvec=cvec, wstream=wstream, adaw=adaw, vecs=vecs, consts=constants(), rope=rope(),
                poolw=poolw, sguw=sguw, rows=rows)


def constants():
    i = np.arange(P)
    rot = np.zeros((P, P), np.float32)
    for p in range(P):
        if p % 32 < 16:
            rot[p + 16, p] = -1.0
        else:
            rot[p - 16, p] = 1.0
    rc = np.zeros((P, 64), np.float32)
    for g, w in enumerate(POOL_W):
        rc[:, 16 * g:16 * (g + 1)] = 1.0 / np.minimum(np.arange(16) + 1, w)
    late = (i[:, None] > i[None, :]).astype(np.float32)
    return np.concatenate([
        np.eye(P), np.ones((P, P)), (i[:, None] // HD == i[None, :] // HD), rot, BIG * late, BIG * late.T,
        (i[:, None] <= i[None, :]), rc], 1).astype(np.float32)


def rope():
    half = HD // 2
    inv = np.float32(10000.0) ** (-np.arange(0, half, 2, dtype=np.float32) / np.float32(half))
    t = np.arange(NX)
    row, col = (t // GRID_W).astype(np.float32), (t % GRID_W).astype(np.float32)
    ang = np.concatenate([row[:, None] * inv, col[:, None] * inv], -1).astype(np.float32)
    out = np.zeros((P, 2, NX), np.float32)
    for p in range(P):
        f = p % HD
        c = (f // half) * (half // 2) + f % (half // 2)
        out[p, 0], out[p, 1] = np.cos(ang[:, c]), np.sin(ang[:, c])
    return out


_INS = ["xin", "cvec", "wstream", "adaw", "vecs", "consts", "rope", "poolw", "sguw", "rows"]


def program(nc, arrays):
    args = [nc.dram_tensor(f"{n}_dram", arrays[f"{n}_dram"].shape, F32, kind="ExternalInput").ap() for n in _INS]
    out = nc.dram_tensor("out_dram", (P, KD, NX), F32, kind="ExternalOutput").ap()
    build(nc, *args, out)


def kernel(**inputs):
    import concourse.bacc as _bacc
    from concourse.bass_utils import run_bass_kernel_spmd as _run

    nc = _bacc.Bacc("TRN2", target_bir_lowering=False, num_devices=1)
    packed = pack(inputs)
    arrays = {f"{n}_dram": np.ascontiguousarray(packed[n]) for n in _INS}
    program(nc, arrays)
    r = _run(nc, [arrays], core_ids=[0])
    got = np.asarray(r.results[0]["out_dram"])
    return np.ascontiguousarray(got.transpose(2, 1, 0).reshape(1, NX, D))
```

```python
from contextlib import ExitStack

import numpy as np

import concourse.bass as bass
from concourse import mybir

ALU = mybir.AluOpType
ACT = mybir.ActivationFunctionType
AX = mybir.AxisListType
F32 = mybir.dt.float32
F32R = mybir.dt.float32r

P = 128
D = 1024
KD = D // P
NC, NX = 256, 512
NT = NC + NX
TT = NT // P
MH, DK, DV = 4, 64, 128
SCW = 512
HID = 4096
AH, KVH, HD = 16, 4, 64
FF = 2816
SGH = 4
GRID_W = 64
POOL_W = (2, 4, 8, 16)
EPS, LN_EPS = 1e-6, 1e-5
ALPHA = (2.0 * 2) ** 0.25
BIG = 1e30
GW = 36
PADW = NT + 4

N_HYB, N_OUT, N_MLP, N_ATT, N_MIX = 25, 8, 64, 12, 12
CH = 8
T_HYB = 0
T_HOUT = T_HYB + N_HYB
T_MLP0 = T_HOUT + N_OUT
T_ATT = T_MLP0 + N_MLP
T_AOUT = T_ATT + N_ATT
T_MLP1 = T_AOUT + N_OUT
T_S = T_MLP1 + N_MLP
NF = FF // P
N_FF = 2 * NF + 3 * KD
N_S = N_MIX + N_OUT + N_FF
N_UNITS = T_S + 2 * N_S
ADA = 48
N_FIRST = 12

_at = {}
_n = 0
for _name, _w in (("ada_b", 4 * ADA), ("norm1_g", 16), ("norm2_g", 16), ("gate_b", 1), ("mnorm_g", 4),
                  ("conv_w", 12), ("q_g", 1), ("k_g", 1), ("pool_scale", 8), ("ln1_g", 16), ("ln1_b", 16),
                  ("ln2_g", 16), ("ln2_b", 16), ("ff_conv_w", 2 * 3 * NF), ("ff_conv_b", 2 * NF),
                  ("eps", 1), ("ln_eps", 1), ("c", 2 * KD)):
    _at[_name] = _n
    _n += _w
VEC_AT, VEC_N = dict(_at), _n
C_ID, C_ONE, C_BD, C_ROT, C_MF, C_MB, C_TRI, C_RC = [P * i for i in range(8)]
CON_N = 7 * P + 64


class At:

    def __init__(self, c, i=None, s=0):
        self.c, self.i, self.s = c, i, s

    def __add__(self, n):
        return At(self.c + n, self.i, self.s)

    def __mod__(self, n):
        assert self.i is None or self.s % n == 0
        return self.c % n

    def __floordiv__(self, n):
        assert self.i is None or self.s % n == 0
        return At(self.c // n, self.i, self.s // n)

    def times(self, n):
        return At(self.c * n, self.i, self.s * n)

    def value(self):
        return self.c if self.i is None else self.i * self.s + self.c

    def positive(self):
        assert self.i is None or self.c > 0, "a loop's first wait would be for nothing"
        return self.c > 0


def wait(eng, sem, at):
    if not isinstance(at, At):
        at = At(at)
    if at.positive():
        eng.wait_ge(sem, at.value())


def build(nc, xin, cvec, wstream, adaw, firstw, vecs_d, consts_d, rope_d, poolw_d, sguw_d, rows_d, out):
    ctx = ExitStack()
    with ctx:
        def sb(name, shape, dt=F32, where=ctx):
            return where.enter_context(nc.sbuf_tensor(name, shape, dt))

        def sem(name):
            return ctx.enter_context(nc.semaphore(name))

        X = sb("X", [P, KD, NT])
        Wraw = sb("Wraw", [P, 4, D])
        Whi = sb("Whi", [P, 2, D], F32R)
        Wlo = sb("Wlo", [P, 2, D], F32R)
        Araw = sb("Araw", [P, 2, D])
        CB = sb("CB", [P, 2, D])
        VEC = sb("VEC", [P, VEC_N])
        CON = sb("CON", [P, CON_N])
        Junk = sb("Junk", [P, D])
        MOD = sb("MOD", [P, 2, 2, ADA])
        MRAW = sb("MRAW", [P, 2, 2, ADA])
        GAIN = sb("GAIN", [P, 2, 2, 2, KD])
        OFFS = sb("OFFS", [P, 2, KD])
        LNA = sb("LNA", [P, 4, KD])
        SQ = sb("SQ", [P, 2, NT])
        T = sb("T", [P, 2, PADW])
        RS = sb("RS", [P, NT])
        ACOL = sb("ACOL", [P, TT, GW])
        small = sb("small", [P, 56])
        RCOL = small[:, 32:56]
        ident = CON[:, C_ID:C_ID + P]
        ones = CON[:, C_ONE:C_ONE + P]
        blockones = CON[:, C_BD:C_BD + P]
        rotate = CON[:, C_ROT:C_ROT + P]
        mask_f = CON[:, C_MF:C_MF + P]
        mask_b = CON[:, C_MB:C_MB + P]
        tri = CON[:, C_TRI:C_TRI + P]

        hyb = ExitStack()
        HQ = sb("HQ", [P, 2, NT], where=hyb)
        HK = sb("HK", [P, 2, NT], where=hyb)
        p0 = ExitStack()
        FIRST = sb("FIRST", [P, N_FIRST, D], where=p0)
        p0.close()
        HV = sb("HV", [P, TT, MH * DV], where=hyb)
        SO = sb("SO", [P, MH, NT], where=hyb)
        CY = sb("CY", [P, 4, 772], where=hyb)
        RM = sb("RM", [P, NT], where=hyb)
        p1 = ExitStack()
        h0 = [sb("h0_hi", [P, KD, NT], F32R, p1), sb("h0_lo", [P, KD, NT], F32R, p1)]
        rows = [sb(f"rows{i}", [P, NT], where=p1) for i in range(3)]
        p1.close()
        pn = ExitStack()
        NUM = [sb("num_f", [P, MH, NT], where=pn), sb("num_b", [P, MH, NT], where=pn)]
        pn.close()
        p2 = ExitStack()
        mixa = [sb("mixa_hi", [P, 4, NT], F32R, p2), sb("mixa_lo", [P, 4, NT], F32R, p2)]
        Mb = sb("Mb", [P, NT], where=p2)
        MD = sb("MD", [P, NT], where=p2)
        DN = sb("DN", [P, NT], where=p2)
        p3 = ExitStack()
        PW = sum(NT - P * i for i in range(TT))
        PB = sb("PB", [P, 2, PW], where=p3)
        p3.close()
        mixb = [sb("mixb_hi", [P, 4, NT], F32R, p2), sb("mixb_lo", [P, 4, NT], F32R, p2)]
        p2.close()
        hyb.close()

        p4 = ExitStack()
        h1 = [sb("h1_hi", [P, KD, NT], F32R, p4), sb("h1_lo", [P, KD, NT], F32R, p4)]
        hid0 = [sb("hid0_hi", [P, CH, NT], F32R, p4), sb("hid0_lo", [P, CH, NT], F32R, p4)]
        p4.close()

        att = ExitStack()
        AQ = sb("AQ", [P, 8, NX], where=att)
        AK = sb("AK", [P, 2, NT], where=att)
        AV = sb("AV", [P, TT, KVH * HD], where=att)
        p5 = ExitStack()
        h2 = [sb("h2_hi", [P, KD, NT], F32R, p5), sb("h2_lo", [P, KD, NT], F32R, p5)]
        ROPE = sb("ROPE", [P, 2, NX], where=p5)
        QN = sb("QN", [P, 2, NT], where=p5)
        RT = sb("RT", [P, NX], where=p5)
        p5.close()
        p6 = ExitStack()
        ao = [sb("ao_hi", [P, KD, NX], F32R, p6), sb("ao_lo", [P, KD, NX], F32R, p6)]
        PR = sb("PR", [P, 2, NT], where=p6)
        PT = sb("PT", [P, 2, TT, NX], where=p6)
        NM = sb("NM", [P, 64], where=p6)
        ZS = sb("ZS", [P, 64], where=p6)
        ZR = sb("ZR", [P, 64], where=p6)
        p6.close()
        att.close()

        p7 = ExitStack()
        h3 = [sb("h3_hi", [P, KD, NX], F32R, p7), sb("h3_lo", [P, KD, NX], F32R, p7)]
        hid1 = [sb("hid1_hi", [P, CH, NX], F32R, p7), sb("hid1_lo", [P, CH, NX], F32R, p7)]
        p7.close()

        p8 = ExitStack()
        hs = [sb("hs_hi", [P, KD, NX], F32R, p8), sb("hs_lo", [P, KD, NX], F32R, p8)]
        p9 = ExitStack()
        ms = [sb("ms_hi", [P, KD, NX], F32R, p9), sb("ms_lo", [P, KD, NX], F32R, p9)]
        PAD = 16
        PA = sb("PA", [P, SGH, PAD + NX], where=p9)
        PS = sb("PS", [P, 2, PAD + NX], where=p9)
        PO = sb("PO", [P, NX], where=p9)
        UG = sb("UG", [P, SGH, NX], where=p9)
        VT = sb("VT", [P, 4, NX], where=p9)
        SW = sb("SW", [P, SGH, P], where=p9)
        POW = sb("POW", [P, SGH, P], where=p9)
        ROW = sb("ROW", [P, 3, NX], where=p9)
        p9.close()
        hid2 = [sb("hid2_hi", [P, CH, NX], F32R, p8), sb("hid2_lo", [P, CH, NX], F32R, p8)]
        GP = sb("GP", [P, 2, 2 + NX], where=p8)
        CV = sb("CV", [P, 2, NX], where=p8)
        p8.close()

        G = [ctx.enter_context(nc.psum_tensor(f"G{i}", [P, 1024], F32)) for i in range(2)]
        B4 = ctx.enter_context(nc.psum_tensor("B4", [P, 1024], F32))
        B6 = ctx.enter_context(nc.psum_tensor("B6", [P, 1024], F32))

        def ps(bank, a, b):
            return bank[:, NC + a:NC + b]

        first_in = [sem(f"first_in{i}") for i in range(N_FIRST // 3)]
        col_sigmoid, col_silu, first_done = map(sem, ("col_sigmoid", "col_silu", "first_done"))
        w_raw = [sem(f"w_raw{i}") for i in range(4)]
        ada_raw = [sem(f"ada_raw{i}") for i in range(2)]
        const_in, c2_in = map(sem, ("const_in", "c2_in"))
        x_in = [sem(f"x_in{i}") for i in range(2)]
        c_in, small_in, late_in, out_dma = map(sem, ("c_in", "small_in", "late_in", "out_dma"))
        w_hi, w_lo, tile_done = map(sem, ("w_hi", "w_lo", "tile_done"))
        tile_free = [sem(f"tile_free{i}") for i in range(2)]
        ada_used, silu_done, silu_ready = map(sem, ("ada_used", "silu_done", "silu_ready"))
        cb_free, mods, vlink = map(sem, ("cb_free", "mods", "vlink"))
        src_ready, hid_ready = map(sem, ("src_ready", "hid_ready"))
        sq_ready, acc_used, std_ready, rstd_ready, nt_ready, nhi_ready = map(
            sem, ("sq_ready", "acc_used", "std_ready", "rstd_ready", "nt_ready", "nhi_ready"))
        col_done, spread_done, var_ready, ln_f_ready = map(sem, ("col_done", "spread_done", "var_ready", "ln_f_ready"))
        gate_step, turned, turn_used = map(sem, ("gate_step", "turned", "turn_used"))
        cu_done, acol_ps, acol_ready = map(sem, ("cu_done", "acol_ps", "acol_ready"))
        m_ps, m_used, md_ready, d_ready, sc_done, p_ready, pv_done, num_used = map(
            sem, ("m_ps", "m_used", "md_ready", "d_ready", "sc_done", "p_ready", "pv_done", "num_used"))
        stab_in, stab_ready, den_read, den_ready, den_spread, den_spread_used, hrstd_ready, chi_ready = map(
            sem, ("stab_in", "stab_ready", "den_read", "den_ready", "den_spread", "den_spread_used", "hrstd_ready",
                  "chi_ready"))
        hsum_ready, hsq_ready, hstat_done, hstd_ready, ht_ready, hhi_ready = map(
            sem, ("hsum_ready", "hsq_ready", "hstat_done", "hstd_ready", "ht_ready", "hhi_ready"))
        hsq2_ready, hidhi_ready = map(sem, ("hsq2_ready", "hidhi_ready"))
        qk_sq, qk_stat, qk_std, qk_n, rot_done, qk_ready = map(
            sem, ("qk_sq", "qk_stat", "qk_std", "qk_n", "rot_done", "qk_ready"))
        as_done, amax_ready, aexp_done, aprob_ready, at_done, at_used, apv_done, ao_hi_ready = map(
            sem, ("as_done", "amax_ready", "aexp_done", "aprob_ready", "at_done", "at_used", "apv_done",
                  "ao_hi_ready"))
        ln_hi_ready, ln_x_ready, ln_t_ready = map(sem, ("ln_hi_ready", "ln_x_ready", "ln_t_ready"))
        pooled, pool_done, v_turned, v_turn_used = map(sem, ("pooled", "pool_done", "v_turned", "v_turn_used"))
        v_var, v_std, v_normed, tri_ready, gated_ps, gated_ready, mix_hi = map(
            sem, ("v_var", "v_std", "v_normed", "tri_ready", "gated_ps", "gated_ready", "mix_hi"))
        ffconv0, ffconv, ffgelu, ffhi = map(sem, ("ffconv0", "ffconv", "ffgelu", "ffhi"))

        FULL, LAT = (0, NT), (NC, NT)

        def parts(rng):
            return [(0, NC), (NC, NT)] if rng == FULL else [(NC, NT)]

        S_N0, S_MIX, S_N1, S_N2, S_AO, S_N3 = range(6)

        def s_set(l, what):
            return 6 + 3 * l + what

        def freed(eng, t):
            wait(eng, tile_free[t % 2], t // 2 + 1)

        def pieces(d):
            out_, at = [], 0
            for i in (0, 1, 2, 3, 4, 5) if d == 0 else (1, 0, 5, 4, 3, 2):
                if i < 2:
                    spans = [(P * i, NC) if d == 0 else (0, P * (i + 1)), (NC, NT)]
                else:
                    spans = [(P * i, NT) if d == 0 else (NC, P * (i + 1))]
                for a, b in spans:
                    out_.append((i, a, b, at))
                    at += b - a
            return out_

        def den_row(h, d):
            return 64 * (h % 2) + 32 * d

        H_M0, H_M1 = 0, 32
        def h_s(l):
            return 64 + NF * l

        block = ctx.enter_context(nc.Block())

        @block.sync
        def _(sp):
            sp.dma_start(VEC[:, :], vecs_d).then_inc(small_in, 16)
            for v in range(2):
                sp.dma_start(CB[:, v, :], cvec[v]).then_inc(c_in, 16)
            for n in range(0, N_FIRST, 3):
                sp.dma_start(FIRST[:, n:n + 3, :], firstw[:, n:n + 3, :]).then_inc(first_in[n // 3], 16)
                if n == 0:
                    sp.dma_start(X[:, 0:4, :], xin[:, 0:4, :]).then_inc(x_in[0], 16)
                if n == 3:
                    sp.dma_start(CON[:, :], consts_d).then_inc(const_in, 16)
                    sp.dma_start(X[:, 4:8, :], xin[:, 4:8, :]).then_inc(x_in[1], 16)

            def load(t):
                wait(sp, w_lo, t + -3)
                s = t % 4
                sp.dma_start(Wraw[:, s, :], wstream[bass.ds(t.value(), 1), :, :].rearrange("a p n -> p (a n)")
                             if t.i is not None else wstream[t.c]).then_inc(w_raw[s], 16)

            def stream(a, b):
                n = (b - a) // 4
                if n > 1:
                    with sp.Fori(0, n) as i:
                        for j in range(4):
                            load(At(a + j, i, 4))
                for u in range(a + (4 * n if n > 1 else 0), b):
                    load(At(u))

            for u in range(4):
                load(At(u))
            stream(4, N_HYB + 1)
            sp.wait_ge(gate_step, 14)
            freed(sp, At(21))
            for h in range(MH):
                for d in range(2):
                    sp.dma_start(T[den_row(h, d):den_row(h, d) + 1, h // 2, 0:NT],
                                 RM[64 + 32 * d + h:65 + 32 * d + h, :]).then_inc(stab_in, 16)
            stream(N_HYB + 1, T_ATT + 4)
            sp.wait_ge(src_ready, 8 * S_N2 + 1)
            sp.dma_start(ROPE[:, :, :], rope_d).then_inc(late_in, 16)
            stream(T_ATT + 4, T_S)
            for l in range(2):
                t0 = T_S + l * N_S
                stream(t0, t0 + 4)
                sp.wait_ge(src_ready, 8 * s_set(l, 0) + 8)
                sp.dma_start(POW[:, :, :], poolw_d[l]).then_inc(late_in, 16)
                sp.dma_start(SW[:, :, :], sguw_d[l]).then_inc(late_in, 16)
                sp.dma_start(ROW[:, :, :], rows_d[l]).then_inc(late_in, 16)
                stream(t0 + 4, t0 + N_S)
            for k in range(KD):
                sp.wait_ge(ln_x_ready, 8 * 3 + k + 1)
                sp.dma_start(out[:, k, :], X[:, k, NC:NT]).then_inc(out_dma, 16)
            sp.wait_ge(out_dma, 16 * KD)

        @block.gpsimd
        def _(pool):
            def load(n):
                wait(pool, ada_used, n + -(N_FIRST + 1))
                pool.dma_start(Araw[:, n % 2, :], adaw[bass.ds(n.value(), 1), :, :].rearrange("a p n -> p (a n)")
                               if n.i is not None else adaw[n.c]).then_inc(ada_raw[n % 2], 16)

            for n in range(2):
                load(At(N_FIRST + n))
            with pool.Fori(0, (2 * ADA - N_FIRST - 2) // 2) as i:
                for j in range(2):
                    load(At(N_FIRST + 2 + j, i, 2))
            pool.wait_ge(cb_free, 1)
            pool.dma_start(CB[:, 0, :], cvec[2]).then_inc(c2_in, 16)
            with pool.Fori(0, ADA) as i:
                for j in range(2):
                    load(At(2 * ADA + j, i, 2))

        @block.tensor
        def _(pe):
            def product(t, src, rng, kt=KD):
                wait(pe, w_lo, t + 1)
                wait(pe, tile_free[t % 2], t // 2)
                s = t % 2
                for a, b in parts(rng):
                    for k in range(kt):
                        hi, lo = src(k)
                        wh, wl = Whi[:, s, k * P:(k + 1) * P], Wlo[:, s, k * P:(k + 1) * P]
                        o = ps(G[s], a, b)
                        pe.matmul(o, wh, hi[:, a:b], start=(k == 0), stop=False)
                        pe.matmul(o, wh, lo[:, a:b], start=False, stop=False)
                        last = pe.matmul(o, wl, hi[:, a:b], start=False, stop=(k == kt - 1))
                last.then_inc(tile_done, 1)

            def first_products(t, src, rng, sem, at, kt=KD, between=None):
                lag = 3 if rng == FULL else 4
                for n in range(kt + lag):
                    if between is not None:
                        between(n)
                    for e, k in ((0, n), (1, n - lag)):
                        if not 0 <= k < kt:
                            continue
                        u = t + e
                        s = u % 2
                        if k == 0:
                            wait(pe, w_lo, u + 1)
                            wait(pe, tile_free[s], u // 2)
                        if e == 0:
                            pe.wait_ge(sem, (at + (k + 1)).value())
                        hi, lo = src(k)
                        wh, wl = Whi[:, s, k * P:(k + 1) * P], Wlo[:, s, k * P:(k + 1) * P]
                        for a, b in parts(rng):
                            o = ps(G[s], a, b)
                            pe.matmul(o, wh, hi[:, a:b], start=(k == 0), stop=False)
                            pe.matmul(o, wh, lo[:, a:b], start=False, stop=False)
                            last = pe.matmul(o, wl, hi[:, a:b], start=False, stop=(k == kt - 1))
                        if k == kt - 1:
                            last.then_inc(tile_done, 1)

            def tiles(pair):
                return lambda k: (pair[0][:, k, :], pair[1][:, k, :])

            def latent(pair):
                class Shifted:
                    def __init__(self, ap):
                        self.ap = ap

                    def __getitem__(self, key):
                        return self.ap[:, key[1].start - NC:key[1].stop - NC]

                return lambda k: (Shifted(pair[0][:, k, :]), Shifted(pair[1][:, k, :]))

            def norm_stats(n, rng, offset=False):
                blocks = range(rng[0] // P, rng[1] // P)
                pe.wait_ge(acc_used, 7 * (n + 1))
                for c in blocks:
                    last = pe.matmul(B4[:, c:c + 1], RS[:, c * P:(c + 1) * P], ones[:, 0:1], start=True, stop=True)
                if offset:
                    for c in blocks:
                        last = pe.matmul(B4[:, 8 + c:9 + c], Junk[:, (c - 2) * P:(c - 1) * P], ones[:, 0:1],
                                         start=True, stop=True)
                last.then_inc(col_done, 1)
                pe.wait_ge(rstd_ready, n + 1)
                for c in blocks:
                    last = pe.matmul(ps(B4, c * P, (c + 1) * P), RCOL[:, c:c + 1].to_broadcast([P, P]), ident,
                                     start=True, stop=True)
                if offset:
                    for c in blocks:
                        last = pe.matmul(ps(B6, c * P, (c + 1) * P), RCOL[:, 8 + c:9 + c].to_broadcast([P, P]), ident,
                                         start=True, stop=True)
                last.then_inc(spread_done, 1)

            def turn(n, first, count):
                freed(pe, At(5 + n if n < 4 else T_ATT + n - 4))
                wait(pe, turn_used, n)
                for i in range(count):
                    last = pe.transpose(B6[:, i * P:(i + 1) * P], T[:, n % 2, first + i * P:first + (i + 1) * P],
                                        ident)
                last.then_inc(turned, 1)

            def mlp(t0, h, hid, rng, sset, h0_):
                src = tiles(h) if rng == FULL else latent(h)
                hsrc = tiles(hid) if rng == FULL else latent(hid)

                def chunk(i):
                    first_products(At(t0, i, 2 * CH), src, rng, src_ready, At(8 * sset))
                    for j in range(2, CH):
                        product(At(t0 + j, i, 2 * CH), src, rng)
                    first_products(At(t0 + CH, i, 2 * CH), hsrc, rng, hid_ready, At(h0_, i, CH))
                    for m in range(2, KD):
                        product(At(t0 + CH + m, i, 2 * CH), hsrc, rng)

                with pe.Fori(0, HID // P // CH) as i:
                    chunk(i)

            pe.wait_ge(col_silu, 1)
            for n in range(N_FIRST):
                if n % 3 == 0:
                    pe.wait_ge(first_in[n // 3], 16)
                for k in range(KD):
                    last = pe.matmul(B6[:, 2 * n:2 * n + 2], FIRST[:, n, k * P:(k + 1) * P], small[:, 2 * k:2 * k + 2],
                                     start=(k == 0), stop=(k == KD - 1))
            last.then_inc(first_done, 1)
            pe.wait_ge(const_in, 16)
            norm_stats(0, FULL)
            src = tiles(h0)
            first_products(At(0), src, FULL, src_ready, At(8 * S_N0))
            for t in range(2, N_HYB):
                product(At(t), src, FULL)
                if 6 <= t < 10:
                    turn(t - 6, 0, TT)
            pe.wait_ge(gate_step, 15)
            for i in range(TT):
                last = pe.transpose(B4[:, i * GW:(i + 1) * GW], rows[1][0:GW, i * P:(i + 1) * P], ident[0:GW, 0:GW])
            last.then_inc(acol_ps, 1)
            def spread_max(q):
                h, d = q // 2, q % 2
                wait(pe, m_used, q)
                wait(pe, den_spread_used, 2 * ((q - 1) // 2 - 1 + (q - 1) % 2))
                wait(pe, hstd_ready, (q - 1) // 2 - 1)
                sel = ident[0:GW, 32 * d + h:32 * d + h + 1].to_broadcast([GW, P])
                for a, b in parts(FULL):
                    last = pe.matmul(ps(B4, a, b), sel, RM[0:GW, a:b], start=True, stop=True)
                last.then_inc(m_ps, 1)

            def spread_den(h, d):
                pe.wait_ge(den_ready, h + 1)
                pe.wait_ge(m_used, min(2 * h + 4, 2 * MH))
                wait(pe, den_spread_used, 2 * h + d)
                r = den_row(h, d)
                for a, b in parts(FULL):
                    last = pe.matmul(ps(B4, a, b), ones[r:r + 1, :], DN[r:r + 1, a:b], start=True, stop=True)
                last.then_inc(den_spread, 1)

            def head_stats(h):
                pe.wait_ge(hsq_ready, h + 1)
                pe.wait_ge(m_used, min(2 * h + 5, 2 * MH))
                for a, b in parts(FULL):
                    last = pe.matmul(ps(B4, a, b), ones, SQ[:, 0, a:b], start=True, stop=True)
                last.then_inc(hstat_done, 1)

            def scores(q, n):
                h, d = q // 2, q % 2
                kb = DK * (h % 2)
                i, a, b, _ = pieces(d)[n]
                r = 8 * q + n
                wait(pe, p_ready, r - 1)
                pe.matmul(G[0][:, 512 * (r % 2):512 * (r % 2) + b - a], HK[kb:kb + DK, h // 2, P * i:P * (i + 1)],
                          HQ[kb:kb + DK, h // 2, a:b], start=True, stop=True).then_inc(sc_done, 1)

            def values(q, n):
                h, d = q // 2, q % 2
                row = den_row(h, d)
                i, a, b, at = pieces(d)[n]
                pe.wait_ge(p_ready, 8 * q + n + 1)
                if n == 0:
                    wait(pe, den_ready, h - 1)
                    wait(pe, num_used, q)
                probs = PB[:, d, at:at + b - a]
                pe.matmul(G[1][row:row + 1, NC + a:NC + b], ones[:, 0:1], probs, start=n in (0, 1), stop=n in (2, 7),
                          skip_group_check=True)
                last = pe.matmul(ps(B6, a, b), HV[:, i, h * DV:(h + 1) * DV], probs, start=n in (0, 1),
                                 stop=n in (2, 7), skip_group_check=True)
                if n == 7:
                    last.then_inc(pv_done, 1)

            pe.wait_ge(acol_ready, 1)
            spread_max(0)
            pe.wait_ge(tile_free[0], (N_HYB + 1) // 2)
            pe.wait_ge(tile_free[1], N_HYB // 2)
            scores(0, 0)
            for q in range(2 * MH):
                h, d = q // 2, q % 2
                for n in range(8):
                    if n < 7:
                        scores(q, n + 1)
                    values(q, n)
                    if n == 1 and q + 1 < 2 * MH:
                        spread_max(q + 1)
                    if h > 0 and d == 0 and n == 5:
                        spread_den(h - 1, 0)
                    if h > 0 and d == 0 and n == 6:
                        spread_den(h - 1, 1)
                    if h > 0 and d == 1 and n == 2:
                        head_stats(h - 1)
                if q + 1 < 2 * MH:
                    scores(q + 1, 0)
            def mixed(k):
                if k < 3 or k == 7:
                    return mixa[0][:, min(k, 3), :], mixa[1][:, min(k, 3), :]
                return mixb[0][:, k - 3, :], mixb[1][:, k - 3, :]

            def last_head(n):
                if n == 2:
                    spread_den(MH - 1, 0)
                if n == 4:
                    spread_den(MH - 1, 1)
                if n == 6:
                    pe.wait_ge(den_spread_used, 2 * MH)
                    head_stats(MH - 1)

            pe.wait_ge(p_ready, 16 * MH)
            pe.wait_ge(den_read, MH)
            first_products(At(T_HOUT), mixed, FULL, src_ready, At(8 * S_MIX), between=last_head)
            for m in range(2, KD):
                product(At(T_HOUT + m), mixed, FULL)
            norm_stats(1, FULL)
            mlp(T_MLP0, h1, hid0, FULL, S_N1, H_M0)
            norm_stats(2, FULL)
            src = tiles(h2)

            def qk_stats(n, rng):
                pe.wait_ge(qk_sq, n + 1)
                wait(pe, qk_std, n)
                for a, b in parts(rng):
                    last = pe.matmul(ps(B4, a, b), blockones, SQ[:, n % 2, a:b], start=True, stop=True)
                last.then_inc(qk_stat, 1)

            def qk_rotate(n):
                pe.wait_ge(qk_n, n + 1)
                wait(pe, qk_ready, n)
                if n == 0:
                    pe.wait_ge(turn_used, 6)
                pe.matmul(B6[:, 0:NX], rotate, QN[:, n % 2, NC:NT], start=True, stop=True).then_inc(rot_done, 1)

            for t in range(N_ATT):
                rng = FULL if t < 4 else LAT
                if t == 0:
                    first_products(At(T_ATT), src, FULL, src_ready, At(8 * S_N2))
                elif t > 1:
                    product(At(T_ATT + t), src, rng)
                if 1 <= t < 3:
                    turn(4 + t - 1, 0, TT)
                if t >= 3:
                    qk_stats(t - 3, FULL if t - 3 < 2 else LAT)
                if t >= 4:
                    qk_rotate(t - 4)
            qk_stats(9, LAT)
            qk_rotate(8)
            qk_rotate(9)
            def score(it):
                j, b, qt = it // 8, it // 2 % 2, 2 * (it // 4 % 2) + it % 2
                kb = HD * b
                if it == 0:
                    pe.wait_ge(qk_ready, 10)
                    pe.wait_ge(tile_free[0], (T_AOUT + 1) // 2)
                    pe.wait_ge(tile_free[1], T_AOUT // 2)
                wait(pe, aexp_done, it - 1)
                q = AQ[kb:kb + HD, j, qt * P:(qt + 1) * P]
                pe.matmul(G[it % 2][:, 0:512], q, AK[kb:kb + HD, j // 4, 0:512], start=True, stop=True)
                pe.matmul(G[it % 2][:, 512:NT], q, AK[kb:kb + HD, j // 4, 512:NT], start=True,
                          stop=True).then_inc(as_done, 1)

            def turn_probs(it):
                pe.wait_ge(aprob_ready, it + 1)
                wait(pe, at_used, it)
                for i in range(TT):
                    last = pe.transpose(B4[:, i * P:(i + 1) * P], PR[:, it % 2, i * P:(i + 1) * P], ident)
                last.then_inc(at_done, 1)

            def attend(r, part):
                j, half = r // 2, r % 2
                if part == 0:
                    pe.wait_ge(at_used, 4 * r + 4)
                    if half == 0 and j > 1:
                        pe.wait_ge(src_ready, 8 * S_AO + j - 1)
                col = 512 * (j % 2) + 2 * P * half
                for n in range(3 * part, 3 * part + 3):
                    i, b = n // 2, n % 2
                    g = 2 * (j // 4) + b
                    last = pe.matmul(B6[HD * b:HD * (b + 1), col:col + 2 * P], AV[:, i, g * HD:(g + 1) * HD],
                                     PT[:, r % 2, i, 2 * P * b:2 * P * (b + 1)], start=(i == 0), stop=(i == TT - 1),
                                     skip_group_check=True)
                if part == 3:
                    last.then_inc(apv_done, 1)

            score(0)
            for it in range(4 * AH):
                if it + 1 < 4 * AH:
                    score(it + 1)
                turn_probs(it)
                if it >= 4:
                    attend(it // 4 - 1, it % 4)
            for part in range(4):
                attend(AH - 1, part)
            pe.wait_ge(aexp_done, 4 * AH)
            src = latent(ao)
            first_products(At(T_AOUT), src, LAT, src_ready, At(8 * S_AO))
            for m in range(2, KD):
                product(At(T_AOUT + m), src, LAT)
            norm_stats(3, LAT)
            mlp(T_MLP1, h3, hid1, LAT, S_N3, H_M1)
            for l in range(2):
                t0 = T_S + l * N_S
                src = latent(hs)

                def pool_product(g):
                    pe.wait_ge(pooled, 4 * l + g + 1)
                    if g == 0:
                        pe.wait_ge(late_in, 16 + 48 * (l + 1))
                        pe.wait_ge(v_turn_used, 4 * l + 4)
                    if g >= 2:
                        pe.wait_ge(src_ready, 8 * s_set(l, 1) + g - 1)
                    pe.matmul(B6[:, 512 * (g % 2):512 * (g % 2) + NX], POW[:, g, :], PO[:, :], start=True,
                              stop=True).then_inc(pool_done, 1)

                def gate_product(h):
                    pe.wait_ge(v_normed, l + 1)
                    pe.wait_ge(tri_ready, l + 1)
                    if h >= 2:
                        pe.wait_ge(gated_ready, 4 * l + h - 1)
                    for c in range(4):
                        last = pe.matmul(B4[:, 512 * (h % 2) + c * P:512 * (h % 2) + (c + 1) * P],
                                         VT[:, c, h * P:(h + 1) * P], SW[:, h, :], start=True, stop=True)
                    last.then_inc(gated_ps, 1)

                for t in range(N_MIX):
                    if t == 0:
                        first_products(At(t0), src, LAT, src_ready, At(8 * s_set(l, 0)))
                    elif t > 1:
                        product(At(t0 + t), src, LAT)
                    if 1 <= t < 5:
                        n = 4 * l + t - 1
                        freed(pe, At(t0 + t - 1))
                        wait(pe, v_turn_used, n)
                        for i in range(4):
                            last = pe.transpose(B6[:, i * P:(i + 1) * P], T[:, n % 2, i * P:(i + 1) * P], ident)
                        last.then_inc(v_turned, 1)
                    if t >= 9:
                        pool_product(t - 9)
                    if t >= 10:
                        gate_product(t - 10)
                pool_product(3)
                gate_product(2)
                gate_product(3)
                src = latent(ms)
                first_products(At(t0 + N_MIX), src, LAT, src_ready, At(8 * s_set(l, 1)))
                for m in range(2, KD):
                    product(At(t0 + N_MIX + m), src, LAT)
                norm_stats(4 + 2 * l, LAT, offset=True)
                t1 = t0 + N_MIX + N_OUT
                src, hsrc = latent(hs), latent(hid2)

                def chunk(i, c0, n_up):
                    first_products(At(t1 + 24 * c0, i, 24), src, LAT, src_ready, At(8 * s_set(l, 2)))
                    for j in range(2, 2 * n_up):
                        product(At(t1 + 24 * c0 + j, i, 24), src, LAT)
                    first_products(At(t1 + 24 * c0 + 2 * n_up, i, 24), hsrc, LAT, hid_ready,
                                   At(h_s(l) + 8 * c0, i, 8), kt=n_up)
                    for m in range(2, KD):
                        product(At(t1 + 24 * c0 + 2 * n_up + m, i, 24), hsrc, LAT, kt=n_up)

                with pe.Fori(0, 2) as i:
                    chunk(i, 0, CH)
                chunk(None, 2, NF - 2 * CH)
                norm_stats(5 + 2 * l, LAT, offset=True)

        @block.scalar
        def _(act):
            def split_hi(t):
                wait(act, w_raw[t % 4], (t // 4 + 1).times(16))
                wait(act, tile_done, t + -1)
                act.activation(Whi[:, t % 2, :], Wraw[:, t % 4, :], ACT.Copy).then_inc(w_hi, 1)

            def evac(t):
                split_hi(t + 2)

            def square(n, k, rng):
                a, b = rng
                if k > 2:
                    act.wait_ge(acc_used, 7 * n + k - 2)
                dst = RS if k == 0 else SQ[:, k % 2, :]
                act.activation(dst[:, a:b], X[:, k, a:b], ACT.Square).then_inc(sq_ready, 1)

            def deviation(n, rng):
                c0, c1 = rng[0] // P, rng[1] // P
                act.wait_ge(col_done, n + 1)
                act.activation(RCOL[:, c0:c1], B4[:, c0:c1], ACT.Sqrt, scale=1.0 / D,
                               bias=VEC[:, VEC_AT["eps"]:VEC_AT["eps"] + 1]).then_inc(std_ready, 1)

            def norm(n, rng, par, which):
                deviation(n, rng)
                dst = (h0, h1, h2, h3)[n]
                off = 0 if n < 3 else NC
                for k in range(KD):
                    act.wait_ge(nt_ready, 8 * n + k + 1)
                    for a, b in parts(rng):
                        v = 1 if a == 0 else 0
                        last = act.activation(dst[0][:, k, a - off:b - off], T[:, k % 2, a:b], ACT.Identity,
                                              bias=MOD[:, par, v, which * 24 + k:which * 24 + k + 1])
                    last.then_inc(nhi_ready, 1)

            def mlp(t0, hid, rng, h0_, after):
                a0, b0 = rng
                off = 0 if rng == FULL else NC

                def chunk(i):
                    for j in range(CH):
                        t = At(t0 + j, i, 16)
                        hn = At(h0_ + j, i, CH)
                        evac(t)
                        act.activation(T[:, j % 2, a0:b0], ps(G[t % 2], a0, b0), ACT.Relu).then_inc(
                            tile_free[t % 2], 1)
                        wait(act, hsq2_ready, hn + 1)
                        act.activation(hid[0][:, j, a0 - off:b0 - off], SQ[:, j % 2, a0:b0],
                                       ACT.Copy).then_inc(hidhi_ready, 1)
                    for m in range(KD):
                        split_hi(At(t0 + CH + m + 2, i, 16))
                        if i is None and m:
                            freed(act, At(t0 + CH + m - 1))
                            after(m - 1)

                n = HID // P // CH - 1
                with act.Fori(0, n) as i:
                    chunk(i)
                t0, h0_ = t0 + 16 * n, h0_ + CH * n
                chunk(None)
                freed(act, At(t0 + 2 * CH - 1))
                after(KD - 1)

            act.wait_ge(small_in, 16)
            act.activation(small[:, 16:16 + 2 * KD], VEC[:, VEC_AT["c"]:VEC_AT["c"] + 2 * KD],
                           ACT.Sigmoid).then_inc(col_sigmoid, 1)
            act.wait_ge(c_in, 32)
            for v in range(2):
                act.activation(SQ[:, v, 0:NT], CB[:, v, 0:NT], ACT.Sigmoid).then_inc(silu_done, 1)
                act.activation(T[:, v, 0:D - NT], CB[:, v, NT:D], ACT.Sigmoid).then_inc(silu_done, 1)
            act.wait_ge(silu_ready, 4)
            for k in range(KD):
                if k % 4 == 0:
                    act.wait_ge(x_in[k // 4], 16)
                if k == 5:
                    split_hi(At(0))
                    split_hi(At(1))
                square(0, k, FULL)
            act.wait_ge(mods, 1)
            norm(0, FULL, 0, 0)
            a, b = FULL
            for t in range(N_HYB):
                evac(At(t))
                g = ps(G[t % 2], a, b)
                if t == 0:
                    gb = VEC_AT["gate_b"]
                    act.activation(rows[0][0:GW, :], g[0:GW, :], ACT.Identity,
                                   bias=VEC[0:GW, gb:gb + 1]).then_inc(gate_step, 1)
                    act.activation(rows[1][0:GW, :], g[64:64 + GW, :], ACT.Identity,
                                   bias=VEC[64:64 + GW, gb:gb + 1]).then_inc(tile_free[0], 1)
                    act.wait_ge(tile_free[0], 1)
                    act.activation(rows[2][0:GW, :], rows[1][0:GW, :], ACT.Abs).then_inc(gate_step, 1)
                    act.wait_ge(gate_step, 2)
                    act.activation(rows[2][0:GW, :], rows[2][0:GW, :], ACT.Exp, scale=-1.0).then_inc(gate_step, 1)
                    act.wait_ge(gate_step, 3)
                    act.activation(rows[2][0:GW, :], rows[2][0:GW, :], ACT.Ln, bias=1.0).then_inc(gate_step, 1)
                elif t < 3:
                    act.activation(HQ[:, t - 1, :], g, ACT.Copy).then_inc(tile_free[t % 2], 1)
                elif t < 5:
                    act.activation(HK[:, t - 3, :], g, ACT.Copy).then_inc(tile_free[t % 2], 1)
                elif t < 9:
                    n = t - 5
                    wait(act, turned, n - 1)
                    act.activation(T[:, n % 2, 0:NT], g, ACT.Copy).then_inc(tile_free[t % 2], 1)
                elif t < 13:
                    act.activation(SO[:, t - 9, :], g, ACT.Sigmoid).then_inc(tile_free[t % 2], 1)
                elif t < 21 and t % 2 == 1:
                    n = (t - 13) // 2
                    wait(act, cu_done, n - 1)
                    act.activation(SQ[:, n % 2, 0:NT], g, ACT.Copy).then_inc(tile_free[1], 1)
            act.wait_ge(acol_ps, 1)
            act.activation(ACOL[:, :, :], B4[:, 0:TT * GW].rearrange("p (i g) -> p i g", g=GW),
                           ACT.Copy).then_inc(acol_ready, 1)
            act.wait_ge(acol_ready, 1)

            def copy_max(q):
                act.wait_ge(m_ps, q + 1)
                wait(act, d_ready, 8 * q)
                wait(act, md_ready, q)
                act.activation(Mb[:, :], ps(B4, 0, NT), ACT.Copy).then_inc(m_used, 1)

            def decays(q):
                h, d = q // 2, q % 2
                act.wait_ge(m_used, q + 1)
                wait(act, pv_done, q - 1)
                for n, (i, a, b, at) in enumerate(pieces(d)):
                    bias = ACOL[:, i, 32 * d + h:32 * d + h + 1]
                    lo_, hi_ = P * i, P * (i + 1)
                    if a <= lo_ and hi_ <= b:
                        segs = [(MD, lo_, hi_)]
                        if a < lo_:
                            segs.append((Mb, a, lo_))
                        if hi_ < b:
                            segs.append((Mb, hi_, b))
                    else:
                        segs = [(Mb, a, b)]
                    if n == 0:
                        act.wait_ge(md_ready, q + 1)
                    for src, u, v in segs:
                        last = act.activation(PB[:, d, at + u - a:at + v - a], src[:, u:v], ACT.Exp, bias=bias,
                                              scale=-1.0)
                    last.then_inc(d_ready, 1)

            def numerator(q):
                act.wait_ge(pv_done, q + 1)
                act.activation(NUM[q % 2][:, q // 2, :], ps(B6, 0, NT), ACT.Copy).then_inc(num_used, 1)

            def head_square(h):
                act.wait_ge(hsum_ready, h + 1)
                act.activation(SQ[:, 0, 0:NT], NUM[1][:, h, :], ACT.Square).then_inc(hsq_ready, 1)

            def head_deviation(h):
                act.wait_ge(hstat_done, h + 1)
                act.activation(RS[:, :], ps(B4, 0, NT), ACT.Sqrt, scale=1.0 / DV,
                               bias=VEC[:, VEC_AT["eps"]:VEC_AT["eps"] + 1]).then_inc(hstd_ready, 1)

            def head_upper(h):
                act.wait_ge(ht_ready, h + 1)
                act.activation(mixa[0][:, h, :], NUM[1][:, h, :], ACT.Copy).then_inc(hhi_ready, 1)

            copy_max(0)
            decays(0)
            act.wait_ge(stab_in, 16 * 2 * MH)
            for h in range(0, MH, 2):
                for e in range(4):
                    r = 32 * e
                    act.activation(T[r:r + 1, h // 2, 0:NT], T[r:r + 1, h // 2, 0:NT], ACT.Exp,
                                   scale=-1.0).then_inc(stab_ready, 1)
            for q in range(2 * MH):
                h, d = q // 2, q % 2
                if q > 0:
                    numerator(q - 1)
                if h > 0 and d == 1:
                    head_square(h - 1)
                if q + 1 < 2 * MH:
                    copy_max(q + 1)
                if h > 0 and d == 1:
                    head_deviation(h - 1)
                if q + 1 < 2 * MH:
                    decays(q + 1)
                if h > 1 and d == 0:
                    head_upper(h - 2)
            numerator(2 * MH - 1)
            head_upper(MH - 2)
            for j in range(4):
                act.activation(mixb[0][:, j, 0:NC], CY[:, j, 1:1 + NC], ACT.Copy)
                act.activation(mixb[0][:, j, NC:NT], CY[:, j, 3 + NC:3 + NT], ACT.Copy).then_inc(chi_ready, 1)
            head_square(MH - 1)
            head_deviation(MH - 1)
            head_upper(MH - 1)
            for m in range(KD):
                split_hi(At(T_HOUT + m + 2))
                if m:
                    freed(act, At(T_HOUT + m - 1))
                    square(1, m - 1, FULL)
            freed(act, At(T_HOUT + KD - 1))
            square(1, KD - 1, FULL)
            norm(1, FULL, 0, 1)
            def last_chunk(k):
                square(2, k, FULL)
                if k == KD - 1:
                    act.wait_ge(c2_in, 16)
                    act.wait_ge(hid_ready, 32)
                    act.activation(T[:, 0, 0:NT], CB[:, 0, 0:NT], ACT.Sigmoid).then_inc(silu_done, 1)
                    act.activation(T[:, 1, 0:D - NT], CB[:, 0, NT:D], ACT.Sigmoid).then_inc(silu_done, 1)

            mlp(T_MLP0, hid0, FULL, H_M0, last_chunk)
            act.wait_ge(mods, 3)
            norm(2, FULL, 1, 0)
            for t in range(N_ATT):
                evac(At(T_ATT + t))
                g = G[(T_ATT + t) % 2]
                if t < 2:
                    n = 4 + t
                    wait(act, turned, n - 1)
                    act.activation(T[:, n % 2, 0:NT], ps(g, 0, NT), ACT.Copy).then_inc(
                        tile_free[(T_ATT + t) % 2], 1)
                else:
                    n = t - 2
                    a, b = FULL if t < 4 else LAT
                    wait(act, qk_n, n - 1)
                    if n < 2:
                        act.wait_ge(turned, 6)
                    act.activation(T[:, n % 2, a:b], ps(g, a, b), ACT.Copy).then_inc(
                        tile_free[(T_ATT + t) % 2], 1)
                    freed(act, At(T_ATT + t))
                    wait(act, qk_stat, n - 1)
                    act.activation(SQ[:, n % 2, a:b], T[:, n % 2, a:b], ACT.Square).then_inc(qk_sq, 1)
                    if n >= 1:
                        a, b = FULL if n - 1 < 2 else LAT
                        act.wait_ge(qk_stat, n)
                        wait(act, qk_n, n - 1)
                        act.activation(RS[:, a:b], ps(B4, a, b), ACT.Sqrt, scale=1.0 / HD,
                                       bias=VEC[:, VEC_AT["eps"]:VEC_AT["eps"] + 1]).then_inc(qk_std, 1)
            act.wait_ge(qk_stat, 10)
            act.wait_ge(qk_n, 9)
            act.activation(RS[:, NC:NT], ps(B4, NC, NT), ACT.Sqrt, scale=1.0 / HD,
                           bias=VEC[:, VEC_AT["eps"]:VEC_AT["eps"] + 1]).then_inc(qk_std, 1)
            act.wait_ge(qk_ready, 10)
            for it in range(4 * AH + 1):
                if it < 4 * AH:
                    act.wait_ge(amax_ready, it + 1)
                    wait(act, at_done, it - 1)
                    act.activation(PR[:, it % 2, :], G[it % 2][:, 0:NT], ACT.Exp, bias=NM[:, it:it + 1],
                                   accum_out=ZS[:, it:it + 1]).then_inc(aexp_done, 1)
                if it >= 1:
                    n = it - 1
                    hn, qt = n // 4, n % 4
                    act.wait_ge(at_done, n + 1)
                    if qt == 0:
                        wait(act, apv_done, hn - 1)
                    act.activation(PT[:, hn % 2, :, qt * P:(qt + 1) * P],
                                   B4[:, 0:NT].rearrange("p (i t) -> p i t", t=P), ACT.Copy).then_inc(at_used, 1)
                    if n % 8 == 6 and n > 8:
                        j = n // 8 - 1
                        act.wait_ge(apv_done, 2 * j + 2)
                        act.activation(ao[0][:, j, :], B6[:, 512 * (j % 2):512 * (j % 2) + NX],
                                       ACT.Copy).then_inc(ao_hi_ready, 1)
            act.wait_ge(apv_done, AH)
            act.activation(ao[0][:, 7, :], B6[:, 512:1024], ACT.Copy).then_inc(ao_hi_ready, 1)
            for m in range(KD):
                split_hi(At(T_AOUT + m + 2))
                if m:
                    freed(act, At(T_AOUT + m - 1))
                    square(3, m - 1, LAT)
            freed(act, At(T_AOUT + KD - 1))
            square(3, KD - 1, LAT)
            norm(3, LAT, 1, 1)

            def enter(k):
                if k == 0:
                    act.wait_ge(mods, 4)
                act.activation(T[:, k % 2, 0:NX], X[:, k, NC:NT], ACT.Identity, scale=GAIN[:, 0, 0, 0, k:k + 1],
                               bias=MOD[:, 0, 0, k:k + 1]).then_inc(ln_f_ready, 1)
                act.activation(hs[0][:, k, :], X[:, k, NC:NT], ACT.Identity, scale=GAIN[:, 0, 0, 0, k:k + 1],
                               bias=MOD[:, 0, 0, k:k + 1]).then_inc(ln_hi_ready, 1)

            mlp(T_MLP1, hid1, LAT, H_M1, enter)
            def layer_norm(n):
                act.wait_ge(var_ready, n + 1)
                act.activation(RCOL[:, 2:6], RCOL[:, 2:6], ACT.Sqrt,
                               bias=VEC[:, VEC_AT["ln_eps"]:VEC_AT["ln_eps"] + 1]).then_inc(std_ready, 1)
                for k in range(KD):
                    act.wait_ge(ln_t_ready, 8 * n + k + 1)
                    if n < 3:
                        scale, bias = GAIN[:, n // 2, 1, n % 2, k:k + 1], OFFS[:, n % 2, k:k + 1]
                        act.activation(hs[0][:, k, :], T[:, k % 2, 0:NX], ACT.Identity, scale=scale,
                                       bias=bias).then_inc(ln_hi_ready, 1)
                        if k >= 2:
                            act.wait_ge(src_ready, 8 * (s_set(n // 2, 2) if n % 2 == 0 else s_set(1, 0)) + k - 1)
                        act.activation(SQ[:, k % 2, 0:NX], T[:, k % 2, 0:NX], ACT.Identity, scale=scale,
                                       bias=bias).then_inc(ln_f_ready, 1)
                    act.activation(X[:, k, NC:NT], T[:, k % 2, 0:NX], ACT.Identity, scale=LNA[:, 0, k:k + 1],
                                   bias=LNA[:, 1, k:k + 1]).then_inc(ln_x_ready, 1)

            for l in range(2):
                t0 = T_S + l * N_S

                def pooled_upper(g):
                    act.wait_ge(pool_done, 4 * l + g + 1)
                    pscale = VEC_AT["pool_scale"] + 4 * l + g
                    act.activation(ms[0][:, g, :], B6[:, 512 * (g % 2):512 * (g % 2) + NX], ACT.Copy,
                                   scale=VEC[:, pscale:pscale + 1]).then_inc(mix_hi, 1)

                for t in range(N_MIX):
                    evac(At(t0 + t))
                    g = ps(G[(t0 + t) % 2], NC, NT)
                    free = tile_free[(t0 + t) % 2]
                    if t < 4:
                        n = 4 * l + t
                        wait(act, v_turned, n - 1)
                        if t == 0:
                            wait(act, ln_x_ready, 16 * l)
                        act.activation(T[:, n % 2, 0:NX], g, ACT.Gelu_apprx_tanh).then_inc(free, 1)
                    elif t < 8:
                        act.activation(PA[:, t - 4, PAD:PAD + NX], g, ACT.Copy).then_inc(free, 1)
                    else:
                        act.activation(UG[:, t - 8, :], g, ACT.Gelu_apprx_tanh).then_inc(free, 1)
                    if t == 6:
                        act.wait_ge(v_var, l + 1)
                        act.activation(small[:, 24:28], small[:, 16:24].rearrange("p (c s) -> p c s", s=2)[:, :, 1],
                                       ACT.Sqrt, bias=VEC[:, VEC_AT["ln_eps"]:VEC_AT["ln_eps"] + 1]).then_inc(v_std, 1)
                    if t >= 9:
                        pooled_upper(t - 9)
                pooled_upper(3)
                for h in range(SGH):
                    act.wait_ge(gated_ready, 4 * l + h + 1)
                    act.activation(ms[0][:, 4 + h, :], T[:, h % 2, 0:NX], ACT.Copy).then_inc(mix_hi, 1)
                for m in range(KD):
                    split_hi(At(t0 + N_MIX + m + 2))
                    if m:
                        freed(act, At(t0 + N_MIX + m - 1))
                        square(4 + 2 * l, m - 1, LAT)
                freed(act, At(t0 + N_MIX + KD - 1))
                square(4 + 2 * l, KD - 1, LAT)
                layer_norm(2 * l)
                t1 = t0 + N_MIX + N_OUT

                def chunk(i, c0, n_up, last=False):
                    for j in range(n_up):
                        t = At(t1 + 24 * c0 + 2 * j, i, 24)
                        fn = At(NF * l + 8 * c0 + j, i, 8)
                        evac(t)
                        act.activation(GP[:, j % 2, 2:2 + NX], ps(G[t % 2], NC, NT), ACT.Copy).then_inc(
                            tile_free[t % 2], 1)
                        wait(act, ffconv, fn.times(2) + 2)
                        act.activation(T[:, j % 2, 0:NX], CV[:, j % 2, :], ACT.Gelu_apprx_tanh).then_inc(ffgelu, 1)
                        split_hi(t + 3)
                        freed(act, t + 1)
                        act.activation(hid2[0][:, j, :], SQ[:, j % 2, 0:NX], ACT.Copy).then_inc(ffhi, 1)
                    for m in range(KD):
                        t = At(t1 + 24 * c0 + 2 * n_up + m, i, 24)
                        if not (last and l == 1 and m >= KD - 2):
                            split_hi(t + 2)
                        if last and m:
                            freed(act, t + -1)
                            square(5 + 2 * l, m - 1, LAT)

                with act.Fori(0, 2) as i:
                    chunk(i, 0, CH)
                chunk(None, 2, NF - 2 * CH, last=True)
                freed(act, At(t0 + N_S - 1))
                square(5 + 2 * l, KD - 1, LAT)
                layer_norm(2 * l + 1)

        @block.vector
        def _(dve):
            links = [0]

            def link(ins):
                links[0] += 1
                ins.then_inc(vlink, 1)
                dve.wait_ge(vlink, links[0])

            def split_lo(t):
                wait(dve, w_hi, t + 1)
                dve.tensor_tensor(Wlo[:, t % 2, :], Wraw[:, t % 4, :], Whi[:, t % 2, :].bitcast(F32),
                                  ALU.subtract).then_inc(w_lo, 1)

            def evac(t):
                split_lo(t + 2)

            def ada(n, col, par, vectors):
                wait(dve, ada_raw[n % 2], (n // 2 + (1 - N_FIRST // 2)).times(16))
                for v in range(vectors):
                    o = MRAW[:, par, v, col.c:col.c + 1] if col.i is None else MRAW[:, par, v, bass.ds(col.value(), 1)]
                    if v + 1 < vectors:
                        wait(dve, ada_used, n + -N_FIRST)
                    products = Araw[:, n % 2, :] if v + 1 == vectors else Junk[:, :]
                    last = dve.scalar_tensor_tensor(out=products, in0=Araw[:, n % 2, :], scalar=1.0, in1=CB[:, v, :],
                                                    op0=ALU.mult, op1=ALU.mult, accum_out=o)
                last.then_inc(ada_used, 1)

            def vec(name, n=0, w=1):
                return VEC[:, VEC_AT[name] + n:VEC_AT[name] + n + w]

            def add_bias(layer, par, vectors, a, b):
                for v in range(vectors):
                    link(dve.tensor_tensor(MOD[:, par, v, a:b], MRAW[:, par, v, a:b], vec("ada_b", ADA * layer + a, b - a),
                                           ALU.add))

            def gains(layer, par, which, vectors):
                for v in range(vectors):
                    link(dve.scalar_tensor_tensor(out=GAIN[:, par, which, v, :],
                                                  in0=MOD[:, par, v, 24 * which + 8:24 * which + 16], scalar=1.0,
                                                  in1=vec(("norm1_g", "norm2_g")[which], 8 * layer, 8),
                                                  op0=ALU.add, op1=ALU.mult))

            def add_squares(n, k, rng, total=False):
                a, b = rng
                wait(dve, sq_ready, 8 * n + k + 1)
                if k == 0:
                    return
                wait(dve, acc_used, 7 * n + k - 1)
                if total:
                    dve.tensor_tensor(Junk[:, 0:NX], X[:, 0, a:b] if k == 1 else Junk[:, 0:NX], X[:, k, a:b], ALU.add)
                dve.tensor_tensor(RS[:, a:b], RS[:, a:b], SQ[:, k % 2, a:b], ALU.add).then_inc(acc_used, 1)

            def norm(n, rng, par, which):
                off = 0 if n < 3 else NC
                dst = (h0, h1, h2, h3)[n]
                c0, c1 = rng[0] // P, rng[1] // P
                dve.wait_ge(std_ready, n + 1)
                dve.reciprocal(RCOL[:, c0:c1], RCOL[:, c0:c1]).then_inc(rstd_ready, 1)
                dve.wait_ge(spread_done, n + 1)

                def scaled(k):
                    wait(dve, nhi_ready, 8 * n + k - 1)
                    wait(dve, src_ready, 8 * (S_N0, S_N1, S_N2, S_N3)[n] + k - 1)
                    for a, b in parts(rng):
                        v = 1 if a == 0 else 0
                        last = dve.scalar_tensor_tensor(out=T[:, k % 2, a:b], in0=X[:, k, a:b],
                                                        scalar=GAIN[:, par, which, v, k:k + 1], in1=ps(B4, a, b),
                                                        op0=ALU.mult, op1=ALU.mult)
                    last.then_inc(nt_ready, 1)

                scaled(0)
                for k in range(KD):
                    if k + 1 < KD:
                        scaled(k + 1)
                    dve.wait_ge(nhi_ready, 8 * n + k + 1)
                    for a, b in parts(rng):
                        v = 1 if a == 0 else 0
                        last = dve.scalar_tensor_tensor(out=dst[1][:, k, a - off:b - off], in0=T[:, k % 2, a:b],
                                                        scalar=MOD[:, par, v, which * 24 + k:which * 24 + k + 1],
                                                        in1=dst[0][:, k, a - off:b - off].bitcast(F32),
                                                        op0=ALU.add, op1=ALU.subtract)
                    last.then_inc(src_ready, 1)

            def add_residual(t, m, rng, par, gate):
                evac(t)
                for a, b in parts(rng):
                    v = 1 if a == 0 else 0
                    last = dve.scalar_tensor_tensor(out=X[:, m, a:b], in0=ps(G[t % 2], a, b),
                                                    scalar=MOD[:, par, v, gate * 8 + m:gate * 8 + m + 1],
                                                    in1=X[:, m, a:b], op0=ALU.mult, op1=ALU.add)
                last.then_inc(tile_free[t % 2], 1)

            def mlp(t0, hid, rng, h0_, par, ada_layer, ada_par, vectors, before, after):
                a0, b0 = rng
                off = 0 if rng == FULL else NC

                def chunk(i, c0):
                    done = 0

                    def step(j):
                        nonlocal done
                        if j < 12 if i is None else j % 4:
                            ada(At(ADA * ada_layer + 12 * c0 + done, i, 12), At(12 * c0 + done, i, 12), ada_par,
                                vectors)
                            done += 1

                    for j in range(CH):
                        t = At(t0 + 16 * c0 + j, i, 16)
                        hn = At(h0_ + CH * c0 + j, i, CH)
                        split_lo(t + 2)
                        step(j)
                        freed(dve, t)
                        dve.tensor_tensor(SQ[:, j % 2, a0:b0], T[:, j % 2, a0:b0], T[:, j % 2, a0:b0],
                                          ALU.mult).then_inc(hsq2_ready, 1)
                        wait(dve, hidhi_ready, hn + 1)
                        dve.tensor_tensor(hid[1][:, j, a0 - off:b0 - off], SQ[:, j % 2, a0:b0],
                                          hid[0][:, j, a0 - off:b0 - off].bitcast(F32),
                                          ALU.subtract).then_inc(hid_ready, 1)
                    for m in range(KD):
                        if i is None:
                            before(m)
                        add_residual(At(t0 + 16 * c0 + CH + m, i, 16), m, rng, par, 5)
                        if i is None and m:
                            after(m - 1)
                        step(CH + m)

                n = HID // P // CH - 1
                with dve.Fori(0, n) as i:
                    chunk(i, 0)
                chunk(None, n)
                after(KD - 1)

            dve.wait_ge(col_sigmoid, 1)
            dve.tensor_tensor(small[:, 0:2 * KD], small[:, 16:16 + 2 * KD], vec("c", 0, 2 * KD),
                              ALU.mult).then_inc(col_silu, 1)
            for v in range(2):
                dve.wait_ge(silu_done, 2 * v + 2)
                dve.tensor_tensor(CB[:, v, 0:NT], CB[:, v, 0:NT], SQ[:, v, 0:NT], ALU.mult).then_inc(silu_ready, 1)
                dve.tensor_tensor(CB[:, v, NT:D], CB[:, v, NT:D], T[:, v, 0:D - NT], ALU.mult).then_inc(silu_ready, 1)
            dve.wait_ge(silu_ready, 4)
            for k in range(KD):
                if k % 2 == 0:
                    ada(At(N_FIRST + k // 2), At(N_FIRST + k // 2), 0, 2)
                if k == KD - 2:
                    split_lo(At(0))
                    split_lo(At(1))
                add_squares(0, k, FULL)
            dve.wait_ge(ada_used, 2 * KD - N_FIRST)
            add_bias(0, 0, 2, N_FIRST, 2 * KD)
            dve.wait_ge(first_done, 1)
            for v in range(2):
                link(dve.tensor_tensor(MOD[:, 0, v, 0:N_FIRST], B6[:, v:2 * N_FIRST:2], vec("ada_b", 0, N_FIRST), ALU.add))
            gains(0, 0, 0, 2)
            dve.sem_inc(mods, 1)
            norm(0, FULL, 0, 0)
            R = [r[0:GW, :] for r in rows]

            def step(ins, n):
                ins.then_inc(gate_step, 1)
                dve.wait_ge(gate_step, n)

            def flip(dst, src, n):
                dve.tensor_copy(dst[0:32, :], src[0:32, :])
                dve.tensor_copy(dst[32:GW, 0:NC], src[32:GW, 0:NC][:, ::-1])
                step(dve.tensor_copy(dst[32:GW, NC:NT], src[32:GW, NC:NT][:, ::-1]), n)

            def gate_chain(part):
                if part == 0:
                    dve.wait_ge(gate_step, 4)
                    step(dve.scalar_tensor_tensor(out=R[1], in0=R[1], scalar=0.0, in1=R[2], op0=ALU.min,
                                                  op1=ALU.subtract), 5)
                    flip(R[2], R[1], 6)
                    step(dve.tensor_tensor_scan(R[1], ones[0:GW, 0:1].to_broadcast([GW, NT]), R[2], 0.0, ALU.mult,
                                                ALU.add), 7)
                    flip(R[2], R[0], 8)
                    step(dve.tensor_tensor(R[2], R[2], R[1], ALU.subtract), 9)
                    step(dve.tensor_tensor_scan(R[0], R[2], R[2], 0.0, ALU.max, ALU.max), 10)
                if part == 1:
                    step(dve.tensor_tensor(R[1], R[1], R[0], ALU.add), 11)
                    flip(RM[0:GW, :], R[0], 12)
                    flip(R[0], R[1], 13)
                    step(dve.tensor_copy(RM[64:64 + GW, :], R[0]), 14)
                    flip(R[1], R[2], 15)

            for t in range(N_HYB):
                if 13 <= t < 21 and t % 2 == 0 or t >= 21:
                    evac(At(t))
                else:
                    split_lo(At(t + 2))
                g = G[t % 2]
                if t in (1, 3):
                    gate_chain(t // 2)
                if 6 <= t < 10:
                    n = t - 6
                    dve.wait_ge(turned, n + 1)
                    dve.tensor_copy(HV[:, :, n * P:(n + 1) * P],
                                    B6[:, 0:NT].rearrange("p (i c) -> p i c", c=P)).then_inc(turn_used, 1)
                if 13 <= t < 21 and t % 2 == 0:
                    j = (t - 13) // 2
                    freed(dve, At(t - 1))
                    if j == 0:
                        dve.wait_ge(turned, 4)
                        link(dve.memset(T[:, 0, :], 0.0))
                    dve.tensor_tensor(T[:, 0, 1:1 + NC], SQ[:, j % 2, 0:NC], ps(g, 0, NC), ALU.mult)
                    link(dve.tensor_tensor(T[:, 0, 3 + NC:3 + NT], SQ[:, j % 2, NC:NT], ps(g, NC, NT), ALU.mult))
                    dve.sem_inc(tile_free[t % 2], 1)
                    dve.sem_inc(cu_done, 1)
                    y = CY[:, j, 1:771]
                    link(dve.tensor_scalar(y, T[:, 0, 0:770], vec("conv_w", j), None, ALU.mult))
                    for k in (1, 2):
                        link(dve.scalar_tensor_tensor(out=y, in0=T[:, 0, k:k + 770], scalar=vec("conv_w", 4 * k + j),
                                                      in1=y, op0=ALU.mult, op1=ALU.add))
                if t >= 21:
                    j = t - 21
                    dve.tensor_tensor(CY[:, j, 1:1 + NC], CY[:, j, 1:1 + NC], ps(g, 0, NC), ALU.mult)
                    link(dve.tensor_tensor(CY[:, j, 3 + NC:3 + NT], CY[:, j, 3 + NC:3 + NT], ps(g, NC, NT), ALU.mult))
                    dve.sem_inc(tile_free[t % 2], 1)
                if t < 16:
                    for n in (16 + 2 * t, 17 + 2 * t):
                        ada(At(n), At(n), 0, 2)
            dve.wait_ge(ada_used, ADA - N_FIRST)
            add_bias(0, 0, 2, 16, ADA)
            gains(0, 0, 1, 2)
            dve.sem_inc(mods, 1)
            def mask_max(q):
                dve.wait_ge(m_used, q + 1)
                wait(dve, d_ready, 8 * q)
                mask = (mask_f, mask_b)[q % 2]
                dve.tensor_tensor(MD[:, :].rearrange("p (i t) -> p i t", t=P), Mb[:, :].rearrange("p (i t) -> p i t", t=P),
                                  mask.unsqueeze(1).broadcast_to([P, TT, P]), ALU.add).then_inc(md_ready, 1)

            def denominator(h):
                r = slice(den_row(h, 0), den_row(h, 1) + 1)
                dve.wait_ge(pv_done, 2 * h + 2)
                dve.wait_ge(stab_ready, 2 * MH)
                wait(dve, den_spread, 2 * h)
                link(dve.tensor_tensor(DN[r, :], G[1][r, NC:NC + NT], T[r, h // 2, 0:NT], ALU.max))
                link(dve.scalar_tensor_tensor(out=DN[r, :], in0=G[1][r, NC:NC + NT], scalar=-1.0, in1=DN[r, :],
                                              op0=ALU.mult, op1=ALU.max))
                dve.sem_inc(den_read, 1)

            def invert_den(h, a, b):
                r = slice(den_row(h, 0), den_row(h, 1) + 1)
                ins = dve.reciprocal(DN[r, a:b], DN[r, a:b])
                if b == NT:
                    ins.then_inc(den_ready, 1)

            def divide(h, d):
                y = NUM[d][:, h, :]
                dve.wait_ge(num_used, 2 * h + 2)
                dve.wait_ge(den_spread, 2 * h + d + 1)
                dve.tensor_tensor(y, y, ps(B4, 0, NT), ALU.mult).then_inc(den_spread_used, 1)
                if d == 1:
                    dve.wait_ge(den_spread_used, 2 * h + 2)
                    dve.tensor_tensor(y, y, NUM[0][:, h, :], ALU.add).then_inc(hsum_ready, 1)

            def invert_std(h, a, b):
                dve.wait_ge(hstd_ready, h + 1)
                dve.reciprocal(RS[:, a:b], RS[:, a:b]).then_inc(hrstd_ready, 1)

            def head_gate(h):
                y = NUM[1][:, h, :]
                link(dve.scalar_tensor_tensor(out=y, in0=y, scalar=vec("mnorm_g", h), in1=RS[:, :], op0=ALU.mult,
                                              op1=ALU.mult))
                dve.tensor_tensor(y, y, SO[:, h, :], ALU.mult).then_inc(ht_ready, 1)

            def head_lower(h):
                dve.wait_ge(hhi_ready, h + 1)
                dve.tensor_tensor(mixa[1][:, h, :], NUM[1][:, h, :], mixa[0][:, h, :].bitcast(F32),
                                  ALU.subtract).then_inc(src_ready, 1)

            part = NT // 4
            mask_max(0)
            for q in range(2 * MH):
                h, d = q // 2, q % 2
                for n, (i, a, b, at) in enumerate(pieces(d)):
                    r = 8 * q + n
                    dve.wait_ge(sc_done, r + 1)
                    dve.wait_ge(d_ready, r + 1)
                    dve.scalar_tensor_tensor(out=PB[:, d, at:at + b - a],
                                             in0=G[0][:, 512 * (r % 2):512 * (r % 2) + b - a], scalar=DK ** -0.5,
                                             in1=PB[:, d, at:at + b - a], op0=ALU.mult, op1=ALU.mult).then_inc(p_ready, 1)
                    if h > 0 and d == 0:
                        if n == 0:
                            denominator(h - 1)
                        elif n < 5:
                            invert_den(h - 1, part * (n - 1), part * n)
                        elif n == 5 and h > 1:
                            head_lower(h - 2)
                        elif n > 5:
                            divide(h - 1, n - 6)
                    if h > 0 and d == 1:
                        if n >= 4:
                            invert_std(h - 1, part * (n - 4), part * (n - 3))
                        if n == 7:
                            dve.wait_ge(hrstd_ready, 4 * h)
                            head_gate(h - 1)
                    if n == 2 and q + 1 < 2 * MH:
                        mask_max(q + 1)
            denominator(MH - 1)
            invert_den(MH - 1, 0, NT)
            head_lower(MH - 2)
            divide(MH - 1, 0)
            for j in range(4):
                dve.wait_ge(chi_ready, j + 1)
                dve.tensor_tensor(mixb[1][:, j, 0:NC], CY[:, j, 1:1 + NC], mixb[0][:, j, 0:NC].bitcast(F32), ALU.subtract)
                dve.tensor_tensor(mixb[1][:, j, NC:NT], CY[:, j, 3 + NC:3 + NT], mixb[0][:, j, NC:NT].bitcast(F32),
                                  ALU.subtract).then_inc(src_ready, 1)
                if j == 1:
                    divide(MH - 1, 1)
            for n in range(4):
                invert_std(MH - 1, part * n, part * (n + 1))
            dve.wait_ge(hrstd_ready, 4 * MH)
            head_gate(MH - 1)
            head_lower(MH - 1)
            for m in range(KD):
                add_residual(At(T_HOUT + m), m, FULL, 0, 2)
                if m:
                    add_squares(1, m - 1, FULL)
            add_squares(1, KD - 1, FULL)
            norm(1, FULL, 0, 1)
            def next_mods(m):
                if m == 5:
                    dve.wait_ge(ada_used, 2 * ADA - N_FIRST)
                    dve.sem_inc(cb_free, 1)
                    add_bias(1, 1, 2, 0, ADA)
                    gains(1, 1, 0, 2)
                    gains(1, 1, 1, 2)
                    dve.sem_inc(mods, 1)

            mlp(T_MLP0, hid0, FULL, H_M0, 0, 1, 1, 2, next_mods, lambda k: add_squares(2, k, FULL))
            dve.wait_ge(silu_done, 6)
            dve.tensor_tensor(CB[:, 0, 0:NT], CB[:, 0, 0:NT], T[:, 0, 0:NT], ALU.mult).then_inc(silu_ready, 1)
            dve.tensor_tensor(CB[:, 0, NT:D], CB[:, 0, NT:D], T[:, 1, 0:D - NT], ALU.mult).then_inc(silu_ready, 1)
            dve.wait_ge(silu_ready, 6)
            norm(2, FULL, 1, 0)

            def qk_finish(n):
                rng = FULL if n < 2 else LAT
                a, b = rng
                dve.wait_ge(qk_std, n + 1)
                link(dve.reciprocal(RS[:, a:b], RS[:, a:b]))
                if n < 2:
                    gain = vec("k_g")
                else:
                    gain = small[:, 0:1]
                wait(dve, rot_done, n - 1)
                dve.scalar_tensor_tensor(out=QN[:, n % 2, a:b], in0=T[:, n % 2, a:b], scalar=gain, in1=RS[:, a:b],
                                         op0=ALU.mult, op1=ALU.mult).then_inc(qk_n, 1)
                dve.wait_ge(qk_n, n + 1)
                if n < 2:
                    dve.tensor_copy(AK[:, n, 0:NC], QN[:, n % 2, 0:NC])

            def qk_turn(n):
                dst = AK[:, n, NC:NT] if n < 2 else AQ[:, n - 2, :]
                link(dve.tensor_tensor(RT[:, :], QN[:, n % 2, NC:NT], ROPE[:, 0, :], ALU.mult))
                dve.wait_ge(rot_done, n + 1)
                link(dve.tensor_tensor(dst, B6[:, 0:NX], ROPE[:, 1, :], ALU.mult))
                dve.tensor_tensor(dst, dst, RT[:, :], ALU.add).then_inc(qk_ready, 1)

            link(dve.tensor_scalar(small[:, 0:1], vec("q_g"), HD ** -0.5, None, ALU.mult))
            for t in range(N_ATT):
                split_lo(At(T_ATT + t + 2))
                if 1 <= t < 3:
                    n = 4 + t - 1
                    dve.wait_ge(turned, n + 1)
                    dve.tensor_copy(AV[:, :, (n - 4) * P:(n - 3) * P],
                                    B6[:, 0:NT].rearrange("p (i c) -> p i c", c=P)).then_inc(turn_used, 1)
                if t == 4:
                    dve.wait_ge(late_in, 16)
                if t >= 3:
                    if t >= 4:
                        qk_turn(t - 4)
                    qk_finish(t - 3)
            qk_turn(8)
            qk_finish(9)
            qk_turn(9)
            for it in range(4 * AH):
                dve.wait_ge(as_done, it + 1)
                dve.tensor_reduce(NM[:, it:it + 1], G[it % 2][:, 0:NT], AX.X, ALU.max, negate=True).then_inc(amax_ready, 1)
                dve.wait_ge(aexp_done, it + 1)
                link(dve.reciprocal(ZR[:, it:it + 1], ZS[:, it:it + 1]))
                dve.tensor_scalar(PR[:, it % 2, :], PR[:, it % 2, :], ZR[:, it:it + 1], None,
                                  ALU.mult).then_inc(aprob_ready, 1)
                if it % 8 == 7 and it > 8:
                    j = it // 8 - 1
                    dve.wait_ge(ao_hi_ready, j + 1)
                    dve.tensor_tensor(ao[1][:, j, :], B6[:, 512 * (j % 2):512 * (j % 2) + NX],
                                      ao[0][:, j, :].bitcast(F32), ALU.subtract).then_inc(src_ready, 1)
            dve.wait_ge(ao_hi_ready, 8)
            dve.tensor_tensor(ao[1][:, 7, :], B6[:, 512:1024], ao[0][:, 7, :].bitcast(F32),
                              ALU.subtract).then_inc(src_ready, 1)
            for m in range(KD):
                add_residual(At(T_AOUT + m), m, LAT, 1, 2)
                if m:
                    add_squares(3, m - 1, LAT)
            add_squares(3, KD - 1, LAT)
            norm(3, LAT, 1, 1)
            def fold(l):
                add_bias(2 + l, l, 1, 0, ADA)
                link(dve.tensor_scalar(GAIN[:, l, 0, 0, :], MOD[:, l, 0, 8:16], 1.0, None, ALU.add))
                link(dve.tensor_scalar(GAIN[:, l, 0, 1, :], MOD[:, l, 0, 32:40], 1.0, None, ALU.add))

            def fold_norm(n, lng, lnb, ln, nxt, which):
                if nxt is not None:
                    scale1, shift = GAIN[:, nxt, 0, which, :], MOD[:, nxt, 0, 24 * which:24 * which + 8]
                    link(dve.tensor_tensor(GAIN[:, n // 2, 1, n % 2, :], scale1, vec(lng, 8 * ln, 8), ALU.mult))
                    link(dve.tensor_tensor(OFFS[:, n % 2, :], scale1, vec(lnb, 8 * ln, 8), ALU.mult))
                    link(dve.tensor_tensor(OFFS[:, n % 2, :], OFFS[:, n % 2, :], shift, ALU.add))
                f = ALPHA if nxt is not None else 1.0
                link(dve.tensor_scalar(LNA[:, 0, :], vec(lng, 8 * ln, 8), f, None, ALU.mult))
                link(dve.tensor_scalar(LNA[:, 1, :], vec(lnb, 8 * ln, 8), f, None, ALU.mult))

            def enter(k):
                dve.wait_ge(ln_f_ready, k + 1)
                dve.wait_ge(ln_hi_ready, k + 1)
                dve.tensor_tensor(hs[1][:, k, :], T[:, k % 2, 0:NX], hs[0][:, k, :].bitcast(F32),
                                  ALU.subtract).then_inc(src_ready, 1)
                dve.tensor_scalar(X[:, k, NC:NT], X[:, k, NC:NT], ALPHA, None, ALU.mult)

            def enter_mods(m):
                if m == 1:
                    dve.wait_ge(ada_used, 2 * ADA + 16 - N_FIRST)
                    add_bias(2, 0, 1, 0, 16)
                    link(dve.tensor_scalar(GAIN[:, 0, 0, 0, :], MOD[:, 0, 0, 8:16], 1.0, None, ALU.add))
                    dve.sem_inc(mods, 1)

            mlp(T_MLP1, hid1, LAT, H_M1, 1, 2, 0, 1, enter_mods, enter)
            dve.wait_ge(ada_used, 3 * ADA - N_FIRST)
            add_bias(2, 0, 1, 16, ADA)
            link(dve.tensor_scalar(GAIN[:, 0, 0, 1, :], MOD[:, 0, 0, 32:40], 1.0, None, ALU.add))
            def layer_norm(n):
                l = n // 2
                mean, sqs = B4[:, 10:14], B4[:, 2:6]
                dve.wait_ge(col_done, 4 + n + 1)
                link(dve.tensor_scalar(RCOL[:, 10:14], mean, 1.0 / D, None, ALU.mult))
                link(dve.tensor_tensor(RCOL[:, 16:20], RCOL[:, 10:14], RCOL[:, 10:14], ALU.mult))
                link(dve.scalar_tensor_tensor(out=RCOL[:, 2:6], in0=sqs, scalar=1.0 / D, in1=RCOL[:, 16:20], op0=ALU.mult,
                                              op1=ALU.subtract))
                dve.tensor_scalar(RCOL[:, 2:6], RCOL[:, 2:6], 0.0, None, ALU.max).then_inc(var_ready, 1)
                dve.wait_ge(std_ready, 4 + n + 1)
                link(dve.reciprocal(RCOL[:, 2:6], RCOL[:, 2:6]))
                dve.tensor_tensor(RCOL[:, 10:14], RCOL[:, 10:14], RCOL[:, 2:6], ALU.mult).then_inc(rstd_ready, 1)
                dve.wait_ge(spread_done, 4 + n + 1)

                def scaled(k):
                    wait(dve, ln_x_ready, 8 * n + k - 1)
                    link(dve.tensor_tensor(T[:, k % 2, 0:NX], X[:, k, NC:NT], ps(B4, NC, NT), ALU.mult))
                    dve.tensor_tensor(T[:, k % 2, 0:NX], T[:, k % 2, 0:NX], ps(B6, NC, NT),
                                      ALU.subtract).then_inc(ln_t_ready, 1)

                scaled(0)
                for k in range(KD):
                    if k + 1 < KD:
                        scaled(k + 1)
                    if n < 3:
                        dve.wait_ge(ln_f_ready, 8 + 8 * n + k + 1)
                        dve.wait_ge(ln_hi_ready, 8 + 8 * n + k + 1)
                        dve.tensor_tensor(hs[1][:, k, :], SQ[:, k % 2, 0:NX], hs[0][:, k, :].bitcast(F32),
                                          ALU.subtract).then_inc(src_ready, 1)

            for l in range(2):
                t0 = T_S + l * N_S

                def pool_tokens(g, w):
                    freed(dve, At(t0 + 4 + g))
                    src_ = PA[:, g, :]
                    for e in range(g + 1):
                        link(dve.tensor_tensor(PS[:, e % 2, PAD:], src_[:, PAD:], src_[:, PAD - 2 ** e:PAD + NX - 2 ** e],
                                               ALU.add))
                        src_ = PS[:, e % 2, :]
                    if g:
                        dve.wait_ge(pool_done, 4 * l + g)
                    link(dve.scalar_tensor_tensor(out=PO[:, :], in0=src_[:, PAD:], scalar=1.0 / w, in1=PA[:, g, PAD:],
                                                  op0=ALU.mult, op1=ALU.subtract))
                    link(dve.tensor_tensor(small[:, 0:16], src_[:, PAD:PAD + 16], CON[:, C_RC + 16 * g:C_RC + 16 * (g + 1)],
                                           ALU.mult))
                    dve.tensor_tensor(PO[:, 0:16], small[:, 0:16], PA[:, g, PAD:PAD + 16], ALU.subtract).then_inc(pooled, 1)

                def pooled_lower(g):
                    dve.wait_ge(mix_hi, 8 * l + g + 1)
                    dve.scalar_tensor_tensor(out=ms[1][:, g, :], in0=B6[:, 512 * (g % 2):512 * (g % 2) + NX],
                                             scalar=vec("pool_scale", 4 * l + g), in1=ms[0][:, g, :].bitcast(F32),
                                             op0=ALU.mult, op1=ALU.subtract).then_inc(src_ready, 1)

                for t in range(N_MIX):
                    split_lo(At(t0 + t + 2))
                    if t == 0:
                        dve.wait_ge(src_ready, 8 * s_set(l, 0) + 8)
                        dve.memset(PA[:, :, 0:PAD], 0.0)
                        dve.memset(PS[:, :, 0:PAD], 0.0)
                        dve.wait_ge(late_in, 16 + 48 * (l + 1))
                        for h in range(SGH):
                            last = dve.tensor_tensor(SW[:, h, :], SW[:, h, :], tri, ALU.mult)
                        last.then_inc(tri_ready, 1)
                    if 1 <= t < 5:
                        n = 4 * l + t - 1
                        dve.wait_ge(v_turned, n + 1)
                        dve.tensor_copy(VT[:, :, (t - 1) * P:t * P],
                                        B6[:, 0:NX].rearrange("p (i c) -> p i c", c=P)).then_inc(v_turn_used, 1)
                    if t == 5:
                        dve.wait_ge(v_turn_used, 4 * l + 4)
                        for c in range(4):
                            link(dve.bn_stats(SQ[:, 0, 8 * c:8 * c + 6], VT[:, c, :]))
                            last = dve.bn_aggr(small[:, 16 + 2 * c:18 + 2 * c], SQ[:, 0, 8 * c:8 * c + 6])
                        last.then_inc(v_var, 1)
                    if t == 6:
                        dve.wait_ge(v_std, l + 1)
                        link(dve.reciprocal(small[:, 28:32], small[:, 24:28]))
                        for c in range(4):
                            link(dve.tensor_scalar(VT[:, c, :], VT[:, c, :], small[:, 16 + 2 * c:17 + 2 * c],
                                                   small[:, 28 + c:29 + c], ALU.subtract, ALU.mult))
                            link(dve.tensor_tensor(VT[:, c, :], VT[:, c, :], ROW[:, 0, :], ALU.mult))
                            link(dve.tensor_tensor(VT[:, c, :], VT[:, c, :], ROW[:, 1, :], ALU.add))
                        dve.sem_inc(v_normed, 1)
                    if t >= 8:
                        pool_tokens(t - 8, POOL_W[t - 8])
                    if t >= 9:
                        pooled_lower(t - 9)
                pooled_lower(3)
                for h in range(SGH):
                    dve.wait_ge(gated_ps, 4 * l + h + 1)
                    freed(dve, At(t0 + 8 + h))
                    bias = ROW[:, 2, h * P:(h + 1) * P].unsqueeze(1).broadcast_to([P, 4, P])
                    link(dve.tensor_tensor(T[:, h % 2, 0:NX].rearrange("p (c t) -> p c t", t=P),
                                           B4[:, 512 * (h % 2):512 * (h % 2) + NX].rearrange("p (c t) -> p c t", t=P),
                                           bias, ALU.add))
                    dve.tensor_tensor(T[:, h % 2, 0:NX], T[:, h % 2, 0:NX], UG[:, h, :], ALU.mult).then_inc(gated_ready, 1)
                    dve.wait_ge(mix_hi, 8 * l + 4 + h + 1)
                    dve.tensor_tensor(ms[1][:, 4 + h, :], T[:, h % 2, 0:NX], ms[0][:, 4 + h, :].bitcast(F32),
                                      ALU.subtract).then_inc(src_ready, 1)
                for m in range(KD):
                    add_residual(At(t0 + N_MIX + m), m, LAT, l, 2)
                    if m:
                        add_squares(4 + 2 * l, m - 1, LAT, total=True)
                    if m == 4:
                        fold_norm(2 * l, "ln1_g", "ln1_b", l, l, 1)
                add_squares(4 + 2 * l, KD - 1, LAT, total=True)
                layer_norm(2 * l)
                t1 = t0 + N_MIX + N_OUT
                dve.wait_ge(tile_done, t1)
                link(dve.memset(GP[:, :, 0:2], 0.0))

                def chunk(i, c0, n_up, last=False):
                    def more(n, count):
                        if l == 0:
                            for e in range(count):
                                ada(At(3 * ADA + n + e, i, 16), At(n + e, i, 16), 1, 1)

                    for j in range(n_up):
                        t = At(t1 + 24 * c0 + 2 * j, i, 24)
                        fn = At(NF * l + 8 * c0 + j, i, 8)
                        split_lo(t + 2)
                        if c0 == 0:
                            more(j, 1)
                        else:
                            more(32 + 2 * j, 2)
                        freed(dve, t)
                        cw = VEC_AT["ff_conv_w"] + 3 * NF * l
                        cb = VEC_AT["ff_conv_b"] + NF * l

                        def col(base):
                            n = base + 8 * c0 + j
                            return VEC[:, n:n + 1] if i is None else VEC[:, bass.ds(i * 8 + n, 1)]

                        y = CV[:, j % 2, :]
                        dve.tensor_scalar(y, GP[:, j % 2, 2:2 + NX], col(cw + 2 * NF), col(cb), ALU.mult,
                                          ALU.add).then_inc(ffconv0, 1)
                        wait(dve, ffconv0, fn + 1)
                        dve.scalar_tensor_tensor(out=y, in0=GP[:, j % 2, 1:1 + NX], scalar=col(cw + NF), in1=y,
                                                 op0=ALU.mult, op1=ALU.add).then_inc(ffconv, 1)
                        wait(dve, ffconv, fn.times(2) + 1)
                        dve.scalar_tensor_tensor(out=y, in0=GP[:, j % 2, 0:NX], scalar=col(cw), in1=y,
                                                 op0=ALU.mult, op1=ALU.add).then_inc(ffconv, 1)
                        split_lo(t + 3)
                        wait(dve, ffgelu, fn + 1)
                        dve.tensor_tensor(SQ[:, j % 2, 0:NX], T[:, j % 2, 0:NX], ps(G[(t + 1) % 2], NC, NT),
                                          ALU.mult).then_inc(tile_free[(t + 1) % 2], 1)
                        wait(dve, ffhi, fn + 1)
                        dve.tensor_tensor(hid2[1][:, j, :], SQ[:, j % 2, 0:NX], hid2[0][:, j, :].bitcast(F32),
                                          ALU.subtract).then_inc(hid_ready, 1)
                    for m in range(KD):
                        t = At(t1 + 24 * c0 + 2 * n_up + m, i, 24)
                        if not (last and l == 1 and m >= KD - 2):
                            split_lo(t + 2)
                        wait(dve, tile_done, t + 1)
                        dve.scalar_tensor_tensor(out=X[:, m, NC:NT], in0=ps(G[t % 2], NC, NT),
                                                 scalar=MOD[:, l, 0, 40 + m:41 + m], in1=X[:, m, NC:NT],
                                                 op0=ALU.mult, op1=ALU.add).then_inc(tile_free[t % 2], 1)
                        if last and m:
                            add_squares(5 + 2 * l, m - 1, LAT, total=True)
                        if c0 == 0:
                            more(8 + m, 1)
                        elif m < 4:
                            more(44 + m, 1)
                        if last and m == 5:
                            if l == 0:
                                dve.wait_ge(ada_used, 4 * ADA - N_FIRST)
                                fold(1)
                                fold_norm(1, "ln2_g", "ln2_b", 0, 1, 0)
                            else:
                                fold_norm(3, "ln2_g", "ln2_b", 1, None, 0)

                with dve.Fori(0, 2) as i:
                    chunk(i, 0, CH)
                chunk(None, 2, NF - 2 * CH, last=True)
                add_squares(5 + 2 * l, KD - 1, LAT, total=True)
                layer_norm(2 * l + 1)


def pack(x):
    f = lambda a: np.ascontiguousarray(np.asarray(a), dtype=np.float32)
    cols = lambda a: f(a).reshape(-1, P).T
    xin = np.concatenate([f(x["ctx"])[0], f(x["x"])[0]], 0)
    xin = f(xin.T.reshape(KD, P, NT).transpose(1, 0, 2))

    def units(w, kt=KD):
        w = f(w)
        if w.shape[0] < KD * P:
            w = np.concatenate([w, np.zeros((KD * P - w.shape[0], w.shape[1]), np.float32)], 0)
        return w.reshape(KD, P, -1, P).transpose(2, 1, 0, 3).reshape(-1, P, KD * P)

    def mlp(w1, w2):
        out = []
        for c in range(HID // D):
            out += [units(w1[:, c * D:(c + 1) * D]), units(w2[c * D:(c + 1) * D])]
        return out

    w = f(x["hyb_w_in"])[0]
    at = np.cumsum([0, 256, 256, 512, 512, 16, 512, 512, 512])
    q, k, v, o, g, gb, gc, u = [w[:, a:b] for a, b in zip(at[:-1], at[1:])]
    gates = np.zeros((D, P), np.float32)
    for n, c in enumerate((0, 64, 32, 96)):
        gates[:, c:c + 4] = g[:, 4 * n:4 * n + 4]
    ws = [units(gates), units(q), units(k), units(v), units(o),
          np.stack([units(gc), units(u)], 1).reshape(-1, P, D), units(gb)]
    rows = np.concatenate([np.arange(0, 3 * P), np.arange(4 * P, D), np.arange(3 * P, 4 * P)])
    ws += [units(f(x["hyb_w_out"])[0][rows])]
    ws += mlp(f(x["mlp_w1"])[0], f(x["mlp_w2"])[0])
    w = f(x["att_w_in"])[0]
    heads = [h for j in range(8) for h in (8 * (j // 4) + j % 4, 8 * (j // 4) + j % 4 + 4)]
    order = np.concatenate([np.arange(HD * h, HD * (h + 1)) for h in heads])
    ws += [units(w[:, 1280:1536]), units(w[:, 1024:1280]), units(w[:, order]), units(f(x["att_w_out"])[0][order])]
    ws += mlp(f(x["mlp_w1"])[1], f(x["mlp_w2"])[1])
    for l in range(2):
        w = f(x["w_in_2"])[l]
        ws += [units(w[:, 1024:1536]), units(w[:, 0:512]), units(w[:, 512:1024]), units(f(x["w_out_2"])[l])]
        up, down = f(x["w_up_2"])[l], f(x["w_down_2"])[l]
        pairs = np.stack([units(up[:, 0:FF]), units(up[:, FF:])], 1)
        for a, b in ((0, 8), (8, 16), (16, NF)):
            ws += [pairs[a:b].reshape(-1, P, D), units(down[a * P:b * P])]
    wstream = np.concatenate(ws, 0)
    assert wstream.shape[0] == N_UNITS
    adaw = np.concatenate([f(x["ada_w"]), f(x["ada_w_2"])], 0).transpose(0, 2, 1).reshape(4 * ADA, P, D)
    firstw = f(units(f(x["ada_w"])[0][:, 0:N_FIRST * P]).transpose(1, 0, 2))
    rep = lambda a: np.broadcast_to(f(a), (P,) + np.shape(a))
    cvec = f(np.stack([rep(x["c"][0]), rep(x["c_ctx"]), rep(x["c_2"][0])], 0))
    gate_b = np.zeros((P, 1), np.float32)
    for n, c in enumerate((0, 64, 32, 96)):
        gate_b[c:c + 4, 0] = f(x["hyb_gate_b"])[0, 4 * n:4 * n + 4]
    vecs = np.concatenate([
        cols(x["ada_b"]), cols(x["ada_b_2"]), cols(x["norm1_g"]), cols(x["norm2_g"]), gate_b,
        cols(x["mlstm_norm_g"]), cols(x["conv_w"]), cols(np.concatenate([f(x["q_norm_g"])[0]] * 2)),
        cols(np.concatenate([f(x["k_norm_g"])[0]] * 2)), cols(x["pool_scale_2"]), cols(x["ln1_g_2"]),
        cols(x["ln1_b_2"]), cols(x["ln2_g_2"]), cols(x["ln2_b_2"]), cols(x["conv_w_2"]), cols(x["conv_b_2"]),
        np.full((P, 1), EPS, np.float32), np.full((P, 1), LN_EPS, np.float32),
        np.stack([cols(x["c"]), cols(x["c_ctx"])], 2).reshape(P, 2 * KD)], 1)
    assert vecs.shape[1] == VEC_N
    poolw = f(x["pool_w_2"]).transpose(0, 2, 1, 3)
    sguw = f(x["sgu_w_2"]).transpose(0, 3, 1, 2)
    rows = np.stack([f(x["sgu_ln_g_2"]), f(x["sgu_ln_b_2"]), f(x["sgu_b_2"]).reshape(2, -1)], 1)
    rows = np.broadcast_to(rows[:, None], (2, P, 3, NX))
    return dict(xin=xin, cvec=cvec, wstream=wstream, adaw=adaw, firstw=firstw, vecs=vecs, consts=constants(), rope=rope(),
                poolw=poolw, sguw=sguw, rows=rows)


def constants():
    i = np.arange(P)
    rot = np.zeros((P, P), np.float32)
    for p in range(P):
        if p % 32 < 16:
            rot[p + 16, p] = -1.0
        else:
            rot[p - 16, p] = 1.0
    rc = np.zeros((P, 64), np.float32)
    for g, w in enumerate(POOL_W):
        rc[:, 16 * g:16 * (g + 1)] = 1.0 / np.minimum(np.arange(16) + 1, w)
    late = (i[:, None] > i[None, :]).astype(np.float32)
    return np.concatenate([
        np.eye(P), np.ones((P, P)), (i[:, None] // HD == i[None, :] // HD), rot, BIG * late, BIG * late.T,
        (i[:, None] <= i[None, :]), rc], 1).astype(np.float32)


def rope():
    half = HD // 2
    inv = np.float32(10000.0) ** (-np.arange(0, half, 2, dtype=np.float32) / np.float32(half))
    t = np.arange(NX)
    row, col = (t // GRID_W).astype(np.float32), (t % GRID_W).astype(np.float32)
    ang = np.concatenate([row[:, None] * inv, col[:, None] * inv], -1).astype(np.float32)
    out = np.zeros((P, 2, NX), np.float32)
    for p in range(P):
        f = p % HD
        c = (f // half) * (half // 2) + f % (half // 2)
        out[p, 0], out[p, 1] = np.cos(ang[:, c]), np.sin(ang[:, c])
    return out


_INS = ["xin", "cvec", "wstream", "adaw", "firstw", "vecs", "consts", "rope", "poolw", "sguw", "rows"]


def program(nc, arrays):
    args = [nc.dram_tensor(f"{n}_dram", arrays[f"{n}_dram"].shape, F32, kind="ExternalInput").ap() for n in _INS]
    out = nc.dram_tensor("out_dram", (P, KD, NX), F32, kind="ExternalOutput").ap()
    build(nc, *args, out)


def kernel(**inputs):
    import concourse.bacc as _bacc
    from concourse.bass_utils import run_bass_kernel_spmd as _run

    nc = _bacc.Bacc("TRN2", target_bir_lowering=False, num_devices=1)
    packed = pack(inputs)
    arrays = {f"{n}_dram": np.ascontiguousarray(packed[n]) for n in _INS}
    program(nc, arrays)
    r = _run(nc, [arrays], core_ids=[0])
    got = np.asarray(r.results[0]["out_dram"])
    return np.ascontiguousarray(got.transpose(2, 1, 0).reshape(1, NX, D))
```
